# Optimizing a Trainium2 kernel written in Bass

```python
import math
import jax
import jax.numpy as jnp
from jax import lax

D_MODEL = 1024
BATCH = 1
SEQ = 512
DEPTH = 2

F32 = jnp.float32
GRID_W = 64
CTX_LEN = 256
N_EVEN = (DEPTH + 1) // 2
N_ODD = DEPTH // 2
DEEPNORM_ALPHA = (2.0 * DEPTH) ** 0.25
DEEPNORM_BETA = (8.0 * DEPTH) ** -0.25
N_MOD = 6
EPS = 1e-6

GDN_HEADS = 4
GDN_DK = 128
GDN_DV = 128
GDN_CONV = 5
GDN_CHUNK = 64
MLA_HEADS = 4
MLA_Q_LORA = 256
MLA_KV_LORA = 256
MLA_NOPE = 128
MLA_ROPE = 64
MLA_DV = 128
Q_BLOCK = 128
ROPE_THETA = 10000.0
NA_HEADS = 8
NA_DH = 64
NA_KH = 8
NA_KW = 16
HG_HEADS = 4
HG_DK = 128
HG_DV = 128
HG_CHUNK = 64
N_EXPERTS = 16
EXPERT_FF = 1024
EC_CAPACITY = 2

GDN_QKV = GDN_HEADS * (2 * GDN_DK + GDN_DV)
EVEN_SPLITS = (GDN_QKV, GDN_HEADS * GDN_DV, 4 * GDN_HEADS, MLA_Q_LORA, MLA_KV_LORA, MLA_ROPE)
EVEN_IN = GDN_QKV + GDN_HEADS * GDN_DV + 4 * GDN_HEADS + MLA_Q_LORA + MLA_KV_LORA + MLA_ROPE
EVEN_MIX = GDN_HEADS * GDN_DV + MLA_HEADS * MLA_DV
NA_QKV = 3 * NA_HEADS * NA_DH
ODD_SPLITS = (NA_QKV, HG_HEADS * HG_DK, HG_HEADS * HG_DK, HG_HEADS * HG_DK, HG_HEADS * HG_DV, HG_HEADS * HG_DV)
ODD_IN = NA_QKV + 3 * HG_HEADS * HG_DK + 2 * HG_HEADS * HG_DV
ODD_MIX = NA_HEADS * NA_DH + HG_HEADS * HG_DV

kernel_name = 'hybrid_diffusion_gdn_mla_na_hgrn2_ec'

def _split(t, sizes):
    out, start = [], 0
    for s in sizes:
        out.append(t[..., start:start + s])
        start += s
    return out

def _heads(t, n_heads):
    B, L, W = t.shape
    return jnp.swapaxes(t.reshape(B, L, n_heads, W // n_heads), 1, 2)

def _flat(t):
    B, L, H, d = t.shape
    return t.reshape(B, L, H * d)

def _rms(x):
    xf = x.astype(F32)
    return (xf * lax.rsqrt(jnp.mean(xf * xf, -1, keepdims=True) + EPS)).astype(x.dtype)

def _l2norm(t):
    tf = t.astype(F32)
    return (tf * lax.rsqrt(jnp.sum(tf * tf, -1, keepdims=True) + EPS)).astype(t.dtype)

def _layer_norm(x, g, b):
    xf = x.astype(F32)
    xc = xf - jnp.mean(xf, -1, keepdims=True)
    y = xc * lax.rsqrt(jnp.mean(xc * xc, -1, keepdims=True) + EPS)
    return y.astype(x.dtype) * g + b

def _gated_rms(o, gain, z):
    B, H, L, d = o.shape
    o = jnp.swapaxes(o, 1, 2)
    return (_rms(o) * gain * jax.nn.silu(z.reshape(B, L, H, d))).reshape(B, L, H * d)

def _short_conv(x, w):
    K, C = w.shape
    pad = K // 2
    return lax.conv_general_dilated(x, w[:, None, :], window_strides=(1,), padding=[(pad, pad)],
                                    dimension_numbers=('NWC', 'WIO', 'NWC'), feature_group_count=C)

def _rope_axis(x, pos):
    half = x.shape[-1] // 2
    inv = ROPE_THETA ** (-jnp.arange(half, dtype=F32) / half)
    ang = pos.astype(F32)[:, None] * inv
    shape = (pos.shape[0],) + (1,) * (x.ndim - 3) + (half,)
    cos, sin = jnp.cos(ang).reshape(shape), jnp.sin(ang).reshape(shape)
    xf = x.astype(F32)
    x1, x2 = xf[..., :half], xf[..., half:]
    return jnp.concatenate([x1 * cos - x2 * sin, x1 * sin + x2 * cos], -1).astype(x.dtype)

def _rope2d(x):
    pos = jnp.arange(x.shape[1])
    half = x.shape[-1] // 2
    return jnp.concatenate([_rope_axis(x[..., :half], pos // GRID_W),
                            _rope_axis(x[..., half:], pos % GRID_W)], -1)

def _softmax_attend(q, k, v, scale):
    s = jnp.einsum('bqhd,bkhd->bhqk', q, k).astype(F32) * scale
    p = jax.nn.softmax(s, axis=-1).astype(v.dtype)
    return jnp.einsum('bhqk,bkhe->bqhe', p, v)

def _blocked_attend(q, k, v, scale):
    B, S, H, d = q.shape
    nb = S // Q_BLOCK
    qb = jnp.moveaxis(q.reshape(B, nb, Q_BLOCK, H, d), 1, 0)
    o = lax.map(lambda qi: _softmax_attend(qi, k, v, scale), qb)
    return jnp.moveaxis(o, 0, 1).reshape(B, S, H, v.shape[-1])

def _gated_delta_chunked(q, k, v, g, beta):
    out_dtype = v.dtype
    q, k, v, g, beta = (t.astype(F32) for t in (q, k, v, g, beta))
    B, H, L, dk = q.shape
    dv = v.shape[-1]
    C = GDN_CHUNK
    N = L // C
    q = (q * dk ** -0.5).reshape(B, H, N, C, dk)
    k = k.reshape(B, H, N, C, dk)
    v = v.reshape(B, H, N, C, dv)
    g = jnp.cumsum(g.reshape(B, H, N, C), axis=-1)
    beta = beta.reshape(B, H, N, C)
    incl = jnp.tril(jnp.ones((C, C), bool))
    strict = jnp.tril(jnp.ones((C, C), bool), -1)
    decay = jnp.exp(jnp.where(incl, g[..., :, None] - g[..., None, :], -jnp.inf))
    k_beta = k * beta[..., None]
    a = jnp.where(strict, jnp.einsum('bhntd,bhnsd->bhnts', k_beta, k) * decay, 0.0)
    rhs = jnp.concatenate([v * beta[..., None], k_beta * jnp.exp(g)[..., None]], -1)
    sol = lax.linalg.triangular_solve(a + jnp.eye(C, dtype=F32), rhs, left_side=True, lower=True,
                                      unit_diagonal=True)
    u, w = sol[..., :dv], sol[..., dv:]
    qk = jnp.einsum('bhntd,bhnsd->bhnts', q, k) * decay
    xs = tuple(jnp.moveaxis(t, 2, 0) for t in (q, k, u, w, g, qk))

    def step(S, inp):
        q_i, k_i, u_i, w_i, g_i, qk_i = inp
        v_new = u_i - jnp.einsum('bhtd,bhde->bhte', w_i, S)
        o = (jnp.einsum('bhtd,bhde->bhte', q_i * jnp.exp(g_i)[..., None], S)
             + jnp.einsum('bhts,bhse->bhte', qk_i, v_new))
        g_last = g_i[..., -1:]
        S = (S * jnp.exp(g_last)[..., None]
             + jnp.einsum('bhsd,bhse->bhde', k_i * jnp.exp(g_last - g_i)[..., None], v_new))
        return S, o

    _, o = lax.scan(step, jnp.zeros((B, H, dk, dv), F32), xs)
    return jnp.moveaxis(o, 0, 2).reshape(B, H, L, dv).astype(out_dtype)

def _gla_chunked(q, v, k, logf):
    out_dtype = v.dtype
    q, v, k, logf = (t.astype(F32) for t in (q, v, k, logf))
    B, H, L, dk = q.shape
    dv = v.shape[-1]
    C = HG_CHUNK
    N = L // C
    G = jnp.cumsum(logf.reshape(B, H, N, C, dk), axis=3)
    xs = tuple(jnp.moveaxis(t, 2, 0) for t in (q.reshape(B, H, N, C, dk), k.reshape(B, H, N, C, dk),
                                                v.reshape(B, H, N, C, dv), G))
    tri = jnp.tril(jnp.ones((C, C), bool))[:, :, None]

    def step(S, inp):
        q_i, k_i, v_i, G_i = inp
        dec = jnp.exp(jnp.where(tri, G_i[:, :, :, None, :] - G_i[:, :, None, :, :], -jnp.inf))
        A = jnp.einsum('bhtd,bhsd,bhtsd->bhts', q_i, k_i, dec)
        o = (jnp.einsum('bhtd,bhde->bhte', q_i * jnp.exp(G_i), S)
             + jnp.einsum('bhts,bhse->bhte', A, v_i))
        G_last = G_i[:, :, -1]
        S = (jnp.exp(G_last)[..., None] * S
             + jnp.einsum('bhsd,bhse->bhde', k_i * jnp.exp(G_last[:, :, None] - G_i), v_i))
        return S, o

    _, o = lax.scan(step, jnp.zeros((B, H, dk, dv), F32), xs)
    return jnp.moveaxis(o, 0, 2).reshape(B, H, L, dv).astype(out_dtype)

def _bidirectional(scan_fn, shared_ctx, shared_lat, dirs_ctx, dirs_lat, need_ctx):
    T = shared_ctx[0].shape[2]
    cat = lambda a, b: jnp.concatenate([a, b], axis=2)
    rev = lambda t: jnp.flip(t, axis=2)
    fwd = scan_fn(*[cat(a, b) for a, b in zip(shared_ctx + dirs_ctx[0], shared_lat + dirs_lat[0])])
    bwd = scan_fn(*[cat(rev(a), rev(b)) for a, b in zip(shared_ctx + dirs_ctx[1], shared_lat + dirs_lat[1])])
    o_lat = fwd[:, :, T:] + rev(bwd[:, :, T:])
    o_ctx = fwd[:, :, :T] + rev(bwd[:, :, :T]) if need_ctx else None
    return o_ctx, o_lat

def _neighbourhood_attend(q, k, v, k_ctx, v_ctx, rpb, scale):
    B, S, H, d = q.shape
    rows = S // GRID_W
    kh, kw = min(NA_KH, rows), NA_KW
    grid = lambda t: t.reshape(B, rows, GRID_W, H, d)
    qg, kg, vg = grid(q), grid(k), grid(v)
    r = jnp.arange(rows)
    row_idx = jnp.clip(r - kh // 2, 0, rows - kh)[:, None] + jnp.arange(kh)[None, :]
    w = jnp.arange(GRID_W)
    c0 = jnp.clip(w - kw // 2, 0, GRID_W - kw)
    col_ok = (w[None, :] >= c0[:, None]) & (w[None, :] < c0[:, None] + kw)
    k_band, v_band = kg[:, row_idx], vg[:, row_idx]
    s_win = jnp.einsum('brwhd,brkchd->bhrwkc', qg, k_band).astype(F32) * scale
    row_off = row_idx - r[:, None] + (NA_KH - 1)
    col_off = jnp.clip(w[None, :] - w[:, None] + (NA_KW - 1), 0, 2 * NA_KW - 2)
    bias = rpb[:, row_off[:, None, :, None], col_off[None, :, None, :]].astype(F32)
    s_win = jnp.where(col_ok[:, None, :], s_win + bias, -jnp.inf)
    s_ctx = jnp.einsum('brwhd,bthd->bhrwt', qg, k_ctx).astype(F32) * scale
    n_win = kh * GRID_W
    p = jax.nn.softmax(jnp.concatenate([s_win.reshape(B, H, rows, GRID_W, n_win), s_ctx], -1), axis=-1)
    p = p.astype(v.dtype)
    p_win = p[..., :n_win].reshape(B, H, rows, GRID_W, kh, GRID_W)
    o = (jnp.einsum('bhrwkc,brkchd->brwhd', p_win, v_band)
         + jnp.einsum('bhrwt,bthd->brwhd', p[..., n_win:], v_ctx))
    return o.reshape(B, S, H * d)

def _expert_choice_ffn(h, w_router, w_gate, w_up, w_down):
    B, N, _ = h.shape
    cap = EC_CAPACITY * N // N_EXPERTS
    aff = jax.nn.softmax(jnp.einsum('bnd,de->bne', h, w_router).astype(F32), axis=-1)
    gate, idx = lax.top_k(jnp.swapaxes(aff, 1, 2), cap)
    bidx = jnp.arange(B)[:, None, None]
    xe = h[bidx, idx]
    hid = jax.nn.silu(jnp.einsum('becd,edf->becf', xe, w_gate)) * jnp.einsum('becd,edf->becf', xe, w_up)
    ye = jnp.einsum('becf,efd->becd', hid, w_down) * gate[..., None].astype(h.dtype)
    return jnp.zeros_like(h).at[bidx, idx].add(ye)

def _even_mixer(u_lat, u_ctx, w_in, conv_w, a_log, dt_bias, gdn_gain, q_gain, kv_gain, w_uq, w_ukv,
                w_out, need_ctx):
    B = u_lat.shape[0]
    p_lat = _split(u_lat @ w_in, EVEN_SPLITS)
    p_ctx = _split(u_ctx @ w_in, EVEN_SPLITS)

    def gdn_prep(p):
        L = p[0].shape[1]
        qkv = jax.nn.silu(_short_conv(p[0], conv_w))
        q, k, v = _split(qkv, (GDN_HEADS * GDN_DK, GDN_HEADS * GDN_DK, GDN_HEADS * GDN_DV))
        q = _l2norm(_heads(q, GDN_HEADS))
        k = _l2norm(_heads(k, GDN_HEADS))
        v = _heads(v, GDN_HEADS)
        ab = jnp.transpose(p[2].astype(F32).reshape(B, L, 2, 2, GDN_HEADS), (2, 3, 0, 4, 1))
        dirs = tuple(
            (-jnp.exp(a_log[d].astype(F32))[:, None] * jax.nn.softplus(ab[0, d] + dt_bias[d].astype(F32)[:, None]),
             jax.nn.sigmoid(ab[1, d]))
            for d in range(2))
        return (q, k, v), dirs

    sh_c, dir_c = gdn_prep(p_ctx)
    sh_l, dir_l = gdn_prep(p_lat)
    gdn_ctx, gdn_lat = _bidirectional(_gated_delta_chunked, sh_c, sh_l, dir_c, dir_l, need_ctx)
    gdn_lat = _gated_rms(gdn_lat, gdn_gain, p_lat[1])

    mla_scale = (MLA_NOPE + MLA_ROPE) ** -0.5

    def mla_kv(p, rotate):
        L = p[4].shape[1]
        kv = ((_rms(p[4]) * kv_gain) @ w_ukv).reshape(B, L, MLA_HEADS, MLA_NOPE + MLA_DV)
        k_rope = _rope2d(p[5]) if rotate else p[5]
        k = jnp.concatenate([kv[..., :MLA_NOPE],
                             jnp.broadcast_to(k_rope[:, :, None, :], (B, L, MLA_HEADS, MLA_ROPE))], -1)
        return k, kv[..., MLA_NOPE:]

    def mla_q(p, rotate):
        L = p[3].shape[1]
        q = ((_rms(p[3]) * q_gain) @ w_uq).reshape(B, L, MLA_HEADS, MLA_NOPE + MLA_ROPE)
        if rotate:
            q = jnp.concatenate([q[..., :MLA_NOPE], _rope2d(q[..., MLA_NOPE:])], -1)
        return q

    k_ctx, v_ctx = mla_kv(p_ctx, False)
    k_lat, v_lat = mla_kv(p_lat, True)
    mla_lat = _blocked_attend(mla_q(p_lat, True), jnp.concatenate([k_ctx, k_lat], 1),
                              jnp.concatenate([v_ctx, v_lat], 1), mla_scale)
    out_lat = jnp.concatenate([gdn_lat, _flat(mla_lat)], -1) @ w_out
    if not need_ctx:
        return out_lat, None
    mla_ctx = _softmax_attend(mla_q(p_ctx, False), k_ctx, v_ctx, mla_scale)
    out_ctx = jnp.concatenate([_gated_rms(gdn_ctx, gdn_gain, p_ctx[1]), _flat(mla_ctx)], -1) @ w_out
    return out_lat, out_ctx

def _odd_mixer(u_lat, u_ctx, w_in, rpb, lb, hg_gain, w_out, need_ctx):
    p_lat = _split(u_lat @ w_in, ODD_SPLITS)
    p_ctx = _split(u_ctx @ w_in, ODD_SPLITS)

    na_scale = NA_DH ** -0.5

    def na_qkv(p):
        B, L, _ = p[0].shape
        return [t.reshape(B, L, NA_HEADS, NA_DH) for t in _split(p[0], (NA_HEADS * NA_DH,) * 3)]

    q_c, k_c, v_c = na_qkv(p_ctx)
    q_l, k_l, v_l = na_qkv(p_lat)
    na_lat = _neighbourhood_attend(q_l, k_l, v_l, k_c, v_c, rpb, na_scale)

    def hg_prep(p):
        q = _heads(jax.nn.silu(p[1]), HG_HEADS)
        v = _heads(p[4], HG_HEADS)
        dirs = []
        for d in range(2):
            z = _heads(p[2 + d], HG_HEADS).astype(F32)
            lbd = lb[d].reshape(1, HG_HEADS, 1, HG_DK)
            logf = jnp.logaddexp(jnp.log(lbd), jnp.log1p(-lbd) + jax.nn.log_sigmoid(z))
            dirs.append(((1.0 - lbd) * jax.nn.sigmoid(-z), logf))
        return (q, v), tuple(dirs)

    sh_c, dir_c = hg_prep(p_ctx)
    sh_l, dir_l = hg_prep(p_lat)
    hg_ctx, hg_lat = _bidirectional(_gla_chunked, sh_c, sh_l, dir_c, dir_l, need_ctx)
    out_lat = jnp.concatenate([na_lat, _gated_rms(hg_lat, hg_gain, p_lat[5])], -1) @ w_out
    if not need_ctx:
        return out_lat, None
    na_ctx = _flat(_softmax_attend(q_c, k_c, v_c, na_scale))
    out_ctx = jnp.concatenate([na_ctx, _gated_rms(hg_ctx, hg_gain, p_ctx[5])], -1) @ w_out
    return out_lat, out_ctx

def setup_inputs(seed: int = 0) -> dict:
    key = jax.random.key(seed)
    ks = jax.random.split(key, 32)
    D = D_MODEL
    nrm = lambda k, shape, s: jax.random.normal(k, shape, F32) * s
    dt = jnp.exp(jax.random.uniform(ks[11], (N_EVEN, 2, GDN_HEADS), F32, math.log(1e-3), math.log(1e-1)))
    return {
        'x': nrm(ks[0], (BATCH, SEQ, D), 1.0),
        'c': nrm(ks[1], (BATCH, D), 1.0),
        'ctx': nrm(ks[2], (BATCH, CTX_LEN, D), 1.0),
        'c_ctx': nrm(ks[3], (D,), 1.0),
        'w_mod': nrm(ks[4], (DEPTH, D, N_MOD * D), 0.5 * D ** -0.5),
        'b_mod': nrm(ks[5], (DEPTH, N_MOD * D), 0.02),
        'ln_g': 1.0 + nrm(ks[6], (DEPTH, 2, D), 0.02),
        'ln_b': nrm(ks[7], (DEPTH, 2, D), 0.02),
        'even_w_in': nrm(ks[8], (N_EVEN, D, EVEN_IN), D ** -0.5),
        'gdn_conv': nrm(ks[9], (N_EVEN, GDN_CONV, GDN_QKV), GDN_CONV ** -0.5),
        'gdn_a_log': jnp.log(jax.random.uniform(ks[10], (N_EVEN, 2, GDN_HEADS), F32, 1.0, 16.0)),
        'gdn_dt_bias': dt + jnp.log(-jnp.expm1(-dt)),
        'gdn_norm': 1.0 + nrm(ks[12], (N_EVEN, GDN_DV), 0.02),
        'mla_q_norm': 1.0 + nrm(ks[13], (N_EVEN, MLA_Q_LORA), 0.02),
        'mla_kv_norm': 1.0 + nrm(ks[14], (N_EVEN, MLA_KV_LORA), 0.02),
        'mla_w_uq': nrm(ks[15], (N_EVEN, MLA_Q_LORA, MLA_HEADS * (MLA_NOPE + MLA_ROPE)), MLA_Q_LORA ** -0.5),
        'mla_w_ukv': nrm(ks[16], (N_EVEN, MLA_KV_LORA, MLA_HEADS * (MLA_NOPE + MLA_DV)), MLA_KV_LORA ** -0.5),
        'even_w_out': nrm(ks[17], (N_EVEN, EVEN_MIX, D), DEEPNORM_BETA * EVEN_MIX ** -0.5),
        'odd_w_in': nrm(ks[18], (N_ODD, D, ODD_IN), D ** -0.5),
        'na_rpb': nrm(ks[19], (N_ODD, NA_HEADS, 2 * NA_KH - 1, 2 * NA_KW - 1), 0.02),
        'hg_lb': nrm(ks[20], (N_ODD, 2, HG_HEADS * HG_DK), 1.0),
        'hg_norm': 1.0 + nrm(ks[21], (N_ODD, HG_DV), 0.02),
        'odd_w_out': nrm(ks[22], (N_ODD, ODD_MIX, D), DEEPNORM_BETA * ODD_MIX ** -0.5),
        'moe_router': nrm(ks[23], (DEPTH, D, N_EXPERTS), D ** -0.5),
        'moe_w_gate': nrm(ks[24], (DEPTH, N_EXPERTS, D, EXPERT_FF), D ** -0.5),
        'moe_w_up': nrm(ks[25], (DEPTH, N_EXPERTS, D, EXPERT_FF), D ** -0.5),
        'moe_w_down': nrm(ks[26], (DEPTH, N_EXPERTS, EXPERT_FF, D), DEEPNORM_BETA * EXPERT_FF ** -0.5),
    }

def reference(x, c, ctx, c_ctx, w_mod, b_mod, ln_g, ln_b, even_w_in, gdn_conv, gdn_a_log, gdn_dt_bias,
              gdn_norm, mla_q_norm, mla_kv_norm, mla_w_uq, mla_w_ukv, even_w_out, odd_w_in, na_rpb, hg_lb,
              hg_norm, odd_w_out, moe_router, moe_w_gate, moe_w_up, moe_w_down):
    lb_all = jnp.cumsum(jax.nn.softmax(hg_lb.astype(F32), axis=0), axis=0)
    lb_all = lb_all - lb_all[:1]
    s_lat = jax.nn.silu(c)
    s_ctx = jax.nn.silu(c_ctx)
    for layer in range(DEPTH):
        j = layer // 2
        need_ctx = layer < DEPTH - 1
        m_lat = jnp.split((s_lat @ w_mod[layer] + b_mod[layer])[:, None, :], N_MOD, axis=-1)
        m_ctx = jnp.split((s_ctx @ w_mod[layer] + b_mod[layer])[None, None, :], N_MOD, axis=-1)
        u_lat = x * (1 + m_lat[1]) + m_lat[0]
        u_ctx = ctx * (1 + m_ctx[1]) + m_ctx[0]
        if layer % 2 == 0:
            o_lat, o_ctx = _even_mixer(u_lat, u_ctx, even_w_in[j], gdn_conv[j], gdn_a_log[j], gdn_dt_bias[j],
                                       gdn_norm[j], mla_q_norm[j], mla_kv_norm[j], mla_w_uq[j], mla_w_ukv[j],
                                       even_w_out[j], need_ctx)
        else:
            o_lat, o_ctx = _odd_mixer(u_lat, u_ctx, odd_w_in[j], na_rpb[j], lb_all[j], hg_norm[j],
                                      odd_w_out[j], need_ctx)
        x = _layer_norm(DEEPNORM_ALPHA * x + m_lat[2] * o_lat, ln_g[layer, 0], ln_b[layer, 0])
        y = _expert_choice_ffn(x * (1 + m_lat[4]) + m_lat[3], moe_router[layer], moe_w_gate[layer],
                               moe_w_up[layer], moe_w_down[layer])
        x = _layer_norm(DEEPNORM_ALPHA * x + m_lat[5] * y, ln_g[layer, 1], ln_b[layer, 1])
        if need_ctx:
            ctx = _layer_norm(DEEPNORM_ALPHA * ctx + m_ctx[2] * o_ctx, ln_g[layer, 0], ln_b[layer, 0])
            y_ctx = _expert_choice_ffn(ctx * (1 + m_ctx[4]) + m_ctx[3], moe_router[layer], moe_w_gate[layer],
                                       moe_w_up[layer], moe_w_down[layer])
            ctx = _layer_norm(DEEPNORM_ALPHA * ctx + m_ctx[5] * y_ctx, ln_g[layer, 1], ln_b[layer, 1])
    return x


_drawn_inputs = setup_inputs


def setup_inputs(seed=0):
    import zlib

    import numpy as np

    out = dict(_drawn_inputs(seed))
    spreads = {}
    factors = {'ctx': 7.044,
     'c_ctx': 3.558,
     'b_mod': 7.625,
     'gdn_a_log': 8.0,
     'gdn_dt_bias': 3.278,
     'gdn_norm': 190.299,
     'mla_q_norm': 8.0,
     'mla_kv_norm': 8.0,
     'mla_w_uq': 8.0,
     'mla_w_ukv': 3.297,
     'na_rpb': 200.0,
     'hg_norm': 154.222}
    for name, (base, spread) in spreads.items():
        noise = np.random.default_rng([zlib.crc32(name.encode()), seed]).standard_normal(out[name].shape)
        drawn = base * np.exp(spread * noise) if base else spread * noise
        out[name] = jnp.asarray(drawn.astype(out[name].dtype))
    for name, factor in factors.items():
        out[name] = (out[name] * factor).astype(out[name].dtype)
    return out
```

```python
import math
from contextlib import ExitStack

import numpy as np

import concourse.bass as bass
from concourse import mybir

F32 = mybir.dt.float32
I32 = mybir.dt.int32
ALU = mybir.AluOpType
ACT = mybir.ActivationFunctionType
AX = mybir.AxisListType

P = 128
D = 1024
KB = D // P
S_LAT, S_CTX = 512, 256
TOK = S_LAT + S_CTX
NT = TOK // P
CT = S_CTX // P
LT = S_LAT // P
H = 4
HW = H * P
DEPTH = 2
NMOD = 6
EPS = 1e-6
ALPHA = (2.0 * DEPTH) ** 0.25
TAPS = 5
ROPE = 64
GRID = 64
ROWS = S_LAT // GRID
NA_H, NA_D = 8, 64
NA_KH, NA_KW = 8, 16
NE = 16
FF = 1024
CAP_L = 2 * S_LAT // NE
CAP_C = 2 * S_CTX // NE
NEG = -1e30
LEVELS = 7
CW = 256
RING = 6
FWD = [0, 1, 2, 3, 4, 5]
BWD = [1, 0, 5, 4, 3, 2]
ORDER = [FWD, BWD]
MOD1_CUTS = (7, 17)
MLA_SCALE = (P + ROPE) ** -0.5
NA_SCALE = NA_D ** -0.5


def shape_constants():
    i = np.arange(P)
    r, c = i[:, None], i[None, :]
    parts = {"ident": r == c, "ones": np.ones((P, P)),
             "incl0": r <= c, "incl1": r >= c, "strict0": r > c, "strict1": r < c}
    for l in range(LEVELS):
        h = 1 << l
        same = r // (2 * h) == c // (2 * h)
        left_right = same & (r // h % 2 == 0) & (c // h % 2 == 1)
        parts[f"level0_{l}"] = left_right
        parts[f"level1_{l}"] = left_right.T
    parts["slots"] = np.tile(np.arange(1, CAP_L + 1), (P, 1))
    parts["slot_lat"] = (i % CAP_L + 1)[:, None]
    parts["slot_ctx"] = (i % CAP_C + 1)[:, None]
    pick = np.zeros((P, NE // 2, P))
    pick_ctx = np.zeros((P, NE // 2, 2 * CAP_C))
    for p in range(NE // 2):
        for e in range(2):
            pick[2 * p + e, p, e * CAP_L:(e + 1) * CAP_L] = 1
            pick_ctx[2 * p + e, p, e * CAP_C:(e + 1) * CAP_C] = 1
    parts["pick_lat"] = pick.reshape(P, -1)
    parts["pick_ctx"] = pick_ctx.reshape(P, -1)
    parts["eps"] = np.full((P, 1), EPS)
    parts["ln_gdn_scale"] = np.full((P, 1), math.log(P ** -0.5))
    half = ROPE // 4
    inv = 10000.0 ** (-np.arange(half, dtype=np.float32) / half)
    t = np.arange(S_LAT)
    ang = np.concatenate([np.tile((t // GRID)[None] * inv[:, None], (2, 1)),
                          np.tile((t % GRID)[None] * inv[:, None], (2, 1))])
    parts["rope_cos"] = np.tile(np.cos(ang), (2, 1))
    parts["rope_sin"] = np.tile(np.sin(ang), (2, 1))
    swap = np.zeros((P, P))
    for b in range(0, P, 2 * half):
        for j in range(half):
            swap[b + half + j, b + j] = -1
            swap[b + j, b + half + j] = 1
    parts["rope_swap"] = swap
    where, cols, at = {}, [], 0
    for name, a in parts.items():
        a = np.asarray(a, np.float32).reshape(P, -1)
        where[name] = (at, at + a.shape[1])
        cols.append(a)
        at += a.shape[1]
    return np.ascontiguousarray(np.concatenate(cols, 1)), where


CONST, CONST_AT = shape_constants()
RESIDENT = CONST_AT["rope_cos"][0]


def program(nc, t, upto=None, dumps=()):
    es = ExitStack()
    with es:
        def sb(name, cols):
            return es.enter_context(nc.sbuf_tensor(name, [P, cols], F32))

        sem_count = [0]

        def sem(name):
            sem_count[0] += 1
            return es.enter_context(nc.semaphore(name))

        ring = sb("ring", RING * KB * CW)
        X = sb("X", NT * D)[:, :].rearrange("p (t d) -> p t d", t=NT)
        cst = sb("cst", RESIDENT)
        small = sb("small", 1600)
        ARENA = 28100
        arena = sb("arena", ARENA)
        bank = [es.enter_context(nc.psum_tensor(f"bank{i}", [P, 512], F32)) for i in range(8)]

        def C(name):
            a, b = CONST_AT[name]
            return cst[:, a:b]

        def A(at, *dims):
            n = int(np.prod(dims))
            assert at + n <= ARENA, (at, dims)
            v = arena[:, at:at + n]
            if len(dims) == 2:
                v = v.rearrange("p (a b) -> p a b", a=dims[0])
            if len(dims) == 3:
                v = v.rearrange("p (a b c) -> p a b c", a=dims[0], b=dims[1])
            return v

        small_at = [0]

        def SM(*dims):
            n = int(np.prod(dims))
            v = small[:, small_at[0]:small_at[0] + n]
            small_at[0] += n
            assert small_at[0] <= 1600
            if len(dims) == 2:
                v = v.rearrange("p (a b) -> p a b", a=dims[0])
            if len(dims) == 3:
                v = v.rearrange("p (a b c) -> p a b c", a=dims[0], b=dims[1])
            return v

        def heads(ap):
            return ap.rearrange("p (h c) -> p h c", h=H)

        def over_heads(mask):
            return mask.rearrange("p (a c) -> p a c", a=1).to_broadcast([P, H, P])

        def over_cols(scalars, n=P):
            k = scalars.shape[1]
            return scalars.rearrange("p (k a) -> p k a", a=1).to_broadcast([scalars.shape[0], k, n])

        ident, ones = C("ident"), C("ones")
        MC = SM(DEPTH, NMOD * KB, 2)
        BMC = SM(DEPTH, NMOD * KB)
        CC = SM(KB, 2)
        COLS = SM(64)
        GQ, GKV = COLS[:, 0:2], COLS[:, 2:4]
        ALOG, DTB = COLS[:, 8:16], COLS[:, 16:24]
        LB, OML, LBX = COLS[:, 24:32], COLS[:, 32:40], COLS[:, 40:48]
        CONVW = SM(12, TAPS)
        ROUT = SM(DEPTH, KB * NE)
        GN = SM(DEPTH, P)
        STAT = SM(NT, 16)
        phase_done = sem("phase_done")
        w_full = [sem(f"w_full{s}") for s in range(RING)]
        dve_step = sem("dve_step")
        act_step = sem("act_step")
        pool_step = sem("pool_step")
        loaded = sem("loaded")
        stored = sem("stored")

        class Chain:

            def __init__(self, s, engine):
                self.s, self.n, self.e = s, 0, engine

            def __call__(self, ins):
                ins.then_inc(self.s, 1)
                self.n += 1
                return ins

            def settle(self):
                if self.n:
                    self.e.wait_ge(self.s, self.n)

            def then(self, ins):
                self(ins)
                self.settle()

        dv, ac, po = Chain(dve_step, nc.vector), Chain(act_step, nc.scalar), Chain(pool_step, nc.gpsimd)

        chunks = []
        experts = []
        released = {}
        n_chunks = [0]

        def chunk(src, k, n):
            chunks.append((n_chunks[0], src, k, n))
            n_chunks[0] += 1
            return n_chunks[0] - 1

        def slot(idx, k=KB, n=CW):
            s = idx % RING
            return ring[:, s * KB * CW:s * KB * CW + k * n].rearrange("p (k n) -> p k n", k=k)

        def wait_chunk(pe, idx):
            pe.wait_ge(w_full[idx % RING], 16 * (idx // RING + 1))

        phases, chunks_until = [], []

        def phase(name, pe=None, act=None, dve=None, pool=None):
            phases.append((name, pe, act, dve, pool))
            chunks_until.append(n_chunks[0])

        calls = {}

        def base(name, n):
            b = calls.get(name, 0)
            calls[name] = b + n
            return b

        def start(mod_pe, mod_act, mod_dve):
            n_load = [0]

            def act():
                def load(dst, src):
                    nc.scalar.dma_start(dst, src).then_inc(loaded, 16)
                    n_load[0] += 16
                for dst, src in ((CC, t["cc"].rearrange("p (k n) -> p k n", k=KB)),
                                 (BMC, t["b_mod_cols"].rearrange("p (l n) -> p l n", l=DEPTH)),
                                 (cst[:, :], t["consts"][:, 0:RESIDENT])):
                    nc.scalar.dma_start(dst, src).then_inc(first_loaded, 16)
                load(X[:, 0:CT, :], t["ctx"].rearrange("o (t p) d -> p (o t) d", p=P))
                load(X[:, CT:NT, :], t["x"].rearrange("o (t p) d -> p (o t) d", p=P))
                load(COLS[:, 0:2], t["q_gain_cols"])
                load(COLS[:, 2:4], t["kv_gain_cols"])
                load(ALOG, t["gdn_a_log"].rearrange("o a b -> o (a b)").to_broadcast([P, 8]))
                load(DTB, t["gdn_dt_bias"].rearrange("o a b -> o (a b)").to_broadcast([P, 8]))
                load(LBX, t["hg_lb_cols"])
                load(CONVW, t["conv_cols"].rearrange("p (k n) -> p k n", k=12))
                for l in range(DEPTH):
                    load(ROUT[:, l, :].rearrange("p (k n) -> p k n", k=KB),
                         t["moe_router"][l].rearrange("(k p) n -> p k n", p=P))
                load(GN[:, 0, :], t["gdn_norm"].to_broadcast([P, P]))
                load(GN[:, 1, :], t["hg_norm"].to_broadcast([P, P]))
                nc.scalar.wait_ge(first_loaded, 48)
                nc.scalar.activation(CC, CC, ACT.Silu).then_inc(silu_c, 1)
                mod_act()
                nc.scalar.wait_ge(loaded, n_load[0])
                nc.scalar.activation(ALOG, ALOG, ACT.Exp)
                nc.scalar.wait_ge(lb_sub, 1)
                nc.scalar.activation(LB, LB, ACT.Exp).then_inc(lb_exp, 1)

            def dve():
                nc.vector.wait_ge(loaded, total_loads_at_start)
                nc.vector.tensor_tensor(LB, LBX, LBX, ALU.subtract).then_inc(lb_sub, 1)
                nc.vector.wait_ge(lb_exp, 1)
                dv.then(nc.vector.reciprocal(OML, LB))
                dv.then(nc.vector.tensor_tensor(LB, LB, OML, ALU.mult))
                dv.then(nc.vector.tensor_tensor(LB, LB, LB, ALU.subtract))
                dv.then(nc.vector.tensor_scalar(OML, LB, -1.0, 1.0, ALU.mult, ALU.add))
                mod_dve()

            phase("mod0", pe=mod_pe, act=act, dve=dve)

        silu_c, lb_sub, lb_exp = sem("silu_c"), sem("lb_sub"), sem("lb_exp")
        first_loaded = sem("first_loaded")
        total_loads_at_start = 16 * 12

        mod_rows, mod_copy, mod_cols, mod_added = (sem(f"mod_{x}") for x in ("rows", "copy", "cols", "added"))

        def modulation(l, lo, hi, banks, at):
            idxs = [chunk(t["w_mod"][l][:, j * CW:(j + 1) * CW], KB, CW) for j in range(lo, hi)]
            b, done = base("mod", hi - lo), base("mod_added", 1)
            for i, idx in enumerate(idxs):
                released[idx] = (mod_rows, b + i + 1)
            ROWS_ = [A(at, CW)[0:2, :], A(at + CW, CW)[0:2, :]]
            cols = bank[banks[2]]
            per = CW // P

            def turn(i):
                nc.tensor.wait_ge(mod_copy, b + i + 1)
                for f in range(per):
                    c = 2 * (per * i + f)
                    mm = nc.tensor.transpose(cols[:, c:c + 2], ROWS_[i % 2][:, f * P:(f + 1) * P], ident[0:2, 0:2])
                mm.then_inc(mod_cols, 1)

            def pe():
                nc.tensor.wait_ge(silu_c, 1)
                for i, idx in enumerate(idxs):
                    wait_chunk(nc.tensor, idx)
                    if i >= 2:
                        nc.tensor.wait_ge(mod_copy, b + i - 1)
                    for k in range(KB):
                        mm = nc.tensor.matmul(bank[banks[i % 2]][0:2, 0:CW], CC[:, k, :], slot(idx)[:, k, :],
                                              start=k == 0, stop=k == KB - 1)
                    mm.then_inc(mod_rows, 1)
                    if i:
                        turn(i - 1)
                turn(len(idxs) - 1)

            def act(share=0, shares=1):
                for i in range(share * len(idxs) // shares, (share + 1) * len(idxs) // shares):
                    nc.scalar.wait_ge(mod_rows, b + i + 1)
                    if i >= 2:
                        nc.scalar.wait_ge(mod_cols, b + i - 1)
                    nc.scalar.activation(ROWS_[i % 2], bank[banks[i % 2]][0:2, 0:CW], ACT.Copy).then_inc(mod_copy, 1)

            def dve():
                nc.vector.wait_ge(mod_cols, b + len(idxs))
                n = per * len(idxs)
                dst = MC[:, l, per * lo:per * hi, :]
                dv.then(nc.vector.tensor_tensor(dst, cols[:, 0:2 * n].rearrange("p (c n) -> p c n", n=2),
                                                over_cols(BMC[:, l, per * lo:per * hi], 2), ALU.add))
                if hi == NMOD * D // CW:
                    for part in (1, 4):
                        v = MC[:, l, part * KB:(part + 1) * KB, :]
                        dv.then(nc.vector.tensor_scalar(v, v, 1.0, None, ALU.add))
                nc.vector.drain().then_inc(mod_added, 1)

            return pe, act, dve, done + 1

        tr_full_l, tr_full_c, tr_done_l, tr_done_c = (sem(f"tr_{x}") for x in ("full_l", "full_c", "done_l", "done_c"))

        def modulated_transpose(l, part_scale, part_shift, with_ctx=True):
            UT = A(0, KB, TOK)
            b = base("tr", KB)
            bc = base("trc", KB) if with_ctx else 0

            def pe():
                for k in range(KB):
                    if k >= 4:
                        nc.tensor.wait_ge(tr_done_l, b + k - 3)
                    for i in range(LT):
                        mm = nc.tensor.transpose(bank[k % 4][:, i * P:(i + 1) * P],
                                                 X[:, CT + i, k * P:(k + 1) * P], ident)
                    mm.then_inc(tr_full_l, 1)
                    if with_ctx:
                        if k >= 4:
                            nc.tensor.wait_ge(tr_done_c, bc + k - 3)
                        for i in range(CT):
                            mm = nc.tensor.transpose(bank[4 + k % 4][:, i * P:(i + 1) * P],
                                                     X[:, i, k * P:(k + 1) * P], ident)
                        mm.then_inc(tr_full_c, 1)

            def act():
                for k in range(KB):
                    nc.scalar.wait_ge(tr_full_l, b + k + 1)
                    nc.scalar.activation(UT[:, k, S_CTX:TOK], bank[k % 4][:, :], ACT.Identity,
                                         bias=MC[:, l, part_shift * KB + k, 0:1],
                                         scale=MC[:, l, part_scale * KB + k, 0:1]).then_inc(tr_done_l, 1)

            def dve():
                if with_ctx:
                    for k in range(KB):
                        nc.vector.wait_ge(tr_full_c, bc + k + 1)
                        nc.vector.tensor_scalar(UT[:, k, 0:S_CTX], bank[4 + k % 4][:, 0:S_CTX],
                                                MC[:, l, part_scale * KB + k, 1:2],
                                                MC[:, l, part_shift * KB + k, 1:2],
                                                ALU.mult, ALU.add).then_inc(tr_done_c, 1)

            phase(f"ut{l}_{part_scale}", pe=pe, act=act, dve=dve)

        pj_full, pj_act, pj_dve = sem("pj_full"), sem("pj_act"), sem("pj_dve")

        def project(name, jobs):
            b = base("pj", len(jobs))
            ba, bd = base("pja", (len(jobs) + 1) // 2), base("pjd", len(jobs) // 2)
            for i, (idx, _, _) in enumerate(jobs):
                released[idx] = (pj_full, b + i + 1)

            def pe():
                for i, (idx, products, evacuate) in enumerate(jobs):
                    if i == 0 or jobs[i - 1][0] != idx:
                        wait_chunk(nc.tensor, idx)
                    if i >= 8:
                        nc.tensor.wait_ge((pj_act, pj_dve)[i % 2], (ba, bd)[i % 2] + (i - 8) // 2 + 1)
                    last = products(bank[i % 8])
                    last.then_inc(pj_full, 1)

            def act():
                for i in range(0, len(jobs), 2):
                    nc.scalar.wait_ge(pj_full, b + i + 1)
                    jobs[i][2](nc.scalar, bank[i % 8]).then_inc(pj_act, 1)

            def dve():
                for i in range(1, len(jobs), 2):
                    nc.vector.wait_ge(pj_full, b + i + 1)
                    jobs[i][2](nc.vector, bank[i % 8]).then_inc(pj_dve, 1)

            phase(name, pe=pe, act=act, dve=dve)

        def evac(dst, rows=slice(0, P)):
            def go(eng, bk):
                src = bk[rows, 0:int(np.prod(dst.shape[1:]))]
                if eng is nc.scalar:
                    return nc.scalar.activation(dst, src, ACT.Copy)
                return nc.vector.tensor_copy(dst, src)
            return go

        def feature_jobs(idx, lhs, rhs, kb, cols, dst, silu=False):
            jobs = []
            for a, b_ in cols:
                def products(bk, a=a, b_=b_):
                    for k in range(kb):
                        mm = nc.tensor.matmul(bk[:, 0:b_ - a], lhs(k), rhs(k, a, b_), start=k == 0, stop=k == kb - 1)
                    return mm
                jobs.append((idx, products, evac(dst(a, b_))))
            return jobs

        ALL = [(0, 384), (384, TOK)]
        LAT = [(S_CTX, TOK)]

        def weights_to_features(src, width, dst, cols, at0=0):
            UT = A(0, KB, TOK)
            jobs = []
            for j in range(width // CW):
                idx = chunk(src[:, j * CW:(j + 1) * CW], KB, CW)
                for f in range(CW // P):
                    jobs += feature_jobs(idx, lambda k, idx=idx, f=f: slot(idx)[:, k, f * P:(f + 1) * P],
                                         lambda k, a, b_: UT[:, k, a:b_], KB, cols,
                                         lambda a, b_, j=j, f=f: dst(j * (CW // P) + f, a, b_))
            return jobs

        def weights_to_tokens(src, width, dst, tiles):
            UT = A(0, KB, TOK)
            jobs = []
            for j in range((width + CW - 1) // CW):
                c0, c1 = j * CW, min(width, (j + 1) * CW)
                idx = chunk(src[:, c0:c1], KB, c1 - c0)
                for tl in tiles:
                    def products(bk, idx=idx, tl=tl, n=c1 - c0):
                        for k in range(KB):
                            mm = nc.tensor.matmul(bk[:, 0:n], UT[:, k, tl * P:(tl + 1) * P],
                                                  slot(idx, KB, n)[:, k, :], start=k == 0, stop=k == KB - 1)
                        return mm
                    jobs.append((idx, products, evac(dst(tl, c0, c1))))
            return jobs

        P34 = A(6144, 4, TOK)
        KR = A(9216, TOK)
        QN = A(9984, H, TOK)
        QR = A(13056, 2, TOK)
        KN = A(14592, H, TOK)
        VM = A(17664, NT, HW)
        MIXM = A(20736, H, TOK)
        ROW = [A(23808, TOK), A(24576, TOK), A(6144, TOK)]
        PT = [A(25344, NT, P), A(26112, NT, P)]
        ROPE_T = A(26880, 1152)
        R_COS, R_SIN, R_SWAP = ROPE_T[:, 0:512], ROPE_T[:, 512:1024], ROPE_T[:, 1024:1152]

        def mla_latents():
            w = t["even_w_in"]
            at = 3 * HW + HW + 16
            UT = A(0, KB, TOK)
            jobs = weights_to_features(w[:, at:at + 2 * CW], 2 * CW, lambda f, a, b: P34[:, f, a:b], ALL)
            idx = chunk(w[:, at + 2 * CW:at + 2 * CW + ROPE], KB, ROPE)
            for rows in (slice(0, ROPE), slice(ROPE, P)):
                for a, b_ in ALL:
                    def products(bk, rows=rows, a=a, b_=b_):
                        for k in range(KB):
                            mm = nc.tensor.matmul(bk[rows, 0:b_ - a], slot(idx, KB, ROPE)[:, k, :], UT[:, k, a:b_],
                                                  start=k == 0, stop=k == KB - 1)
                        return mm
                    jobs.append((idx, products, evac(KR[rows, a:b_], rows=rows)))
            project("mla_latents", jobs)

        bias_in = [sem("bias_in0"), sem("bias_in1")]
        ms_sq, ms_sum, ms_rs, ms_out = (sem(f"ms_{x}") for x in ("sq", "sum", "rs", "out"))

        def mla_norm():
            SQ, RN = A(23808, 2, TOK), A(25344, TOK)

            def act():
                nc.scalar.dma_start(ROPE_T, t["consts"][:, RESIDENT:RESIDENT + 1152]).then_inc(loaded, 16)
                for g in range(2):
                    if g:
                        nc.scalar.wait_ge(ms_sum, 2 * g)
                    nc.scalar.activation(SQ, P34[:, 2 * g:2 * g + 2, :], ACT.Square).then_inc(ms_sq, 1)
                    if g:
                        nc.scalar.wait_ge(ms_out, 2)
                    for n, (a, b_) in enumerate(ALL):
                        nc.scalar.wait_ge(ms_sum, 2 * g + n + 1)
                        ac.then(nc.scalar.activation(RN[:, a:b_], bank[2 * g + n][:, 0:b_ - a], ACT.Ln,
                                                     bias=C("eps"), scale=1.0 / (2 * P)))
                        nc.scalar.activation(RN[:, a:b_], RN[:, a:b_], ACT.Exp, scale=-0.5).then_inc(ms_rs, 1)

            def pe():
                for g in range(2):
                    nc.tensor.wait_ge(ms_sq, g + 1)
                    for n, (a, b_) in enumerate(ALL):
                        for k in range(2):
                            mm = nc.tensor.matmul(bank[2 * g + n][:, 0:b_ - a], ones, SQ[:, k, a:b_], start=k == 0, stop=k == 1)
                        mm.then_inc(ms_sum, 1)

            def dve():
                for g in range(2):
                    nc.vector.wait_ge(ms_rs, 2 * g + 2)
                    for k in range(2):
                        v = P34[:, 2 * g + k, :]
                        nc.vector.scalar_tensor_tensor(v, v, (GQ, GKV)[g][:, k:k + 1], RN, ALU.mult, ALU.mult).then_inc(ms_out, 1)

            phase("mla_norm", pe=pe, act=act, dve=dve)

        def mla_up():
            jobs = []
            QKW = P + ROPE
            iq = chunk(t["mla_w_uq"], 2, H * QKW)
            ik = chunk(t["mla_w_ukv"], 2, H * 2 * P)
            wq, wk = slot(iq, 2, H * QKW), slot(ik, 2, H * 2 * P)
            for h in range(H):
                jobs += feature_jobs(iq, lambda k, h=h: wq[:, k, h * QKW:h * QKW + P], lambda k, a, b_: P34[:, k, a:b_], 2,
                                     ALL, lambda a, b_, h=h: QN[:, h, a:b_])
            for j in range(2):
                for a, b_ in ALL:
                    def products(bk, j=j, a=a, b_=b_):
                        for s in range(2):
                            w0 = (2 * j + s) * QKW + P
                            for k in range(2):
                                mm = nc.tensor.matmul(bk[s * ROPE:(s + 1) * ROPE, 0:b_ - a], wq[:, k, w0:w0 + ROPE],
                                                      P34[:, k, a:b_], start=k == 0, stop=k == 1)
                        return mm
                    jobs.append((iq, products, evac(QR[:, j, a:b_])))
            for h in range(H):
                jobs += feature_jobs(ik, lambda k, h=h: wk[:, k, 2 * h * P:2 * h * P + P],
                                     lambda k, a, b_: P34[:, 2 + k, a:b_], 2, ALL, lambda a, b_, h=h: KN[:, h, a:b_])
            for tl in range(NT):
                def products(bk, tl=tl):
                    for k in range(2):
                        mm = nc.tensor.matmul(bk[:, :], P34[:, 2 + k, tl * P:(tl + 1) * P],
                                              wk[:, k, :].rearrange("p (h c) -> p h c", h=H)[:, :, P:2 * P],
                                              start=k == 0, stop=k == 1)
                    return mm
                jobs.append((ik, products, evac(VM[:, tl, :])))
            project("mla_up", jobs)

        rp_full, rp_tmp, rp_done = sem("rp_full"), sem("rp_tmp"), sem("rp_done")

        def mla_rope():
            rows = [QR[:, 0, S_CTX:TOK], QR[:, 1, S_CTX:TOK], KR[:, S_CTX:TOK]]
            TMP = ROW[0][:, 0:512]

            def pe():
                nc.tensor.wait_ge(loaded, rope_loaded)
                for i, x in enumerate(rows):
                    nc.tensor.matmul(bank[i][:, :], R_SWAP, x, start=True, stop=True).then_inc(rp_full, 1)

            def dve():
                nc.vector.wait_ge(loaded, rope_loaded)
                for i, x in enumerate(rows):
                    nc.vector.wait_ge(rp_full, i + 1)
                    dv.settle()
                    dv.then(nc.vector.tensor_tensor(TMP, bank[i][:, :], R_SIN, ALU.mult))
                    dv.then(nc.vector.tensor_tensor(x, x, R_COS, ALU.mult))
                    dv.then(nc.vector.tensor_tensor(x, x, TMP, ALU.add))

            phase("mla_rope", pe=pe, dve=dve)

        rope_loaded = total_loads_at_start + 16

        at_s, at_neg, at_exp, at_p, at_t, at_pt, at_o, at_oc = (
            sem(f"at_{x}") for x in ("scores", "negmax", "exp", "probs", "turned", "turned_copy", "out", "out_copy"))

        def attention(name, items, row, pt, scale, pool=None):
            b = base("at", len(items))
            MX = SMALL_ATT

            def halves(i):
                at, out = 0, []
                for n, (products, keys) in enumerate(items[i]["scores"]):
                    out.append((bank[4 * (i % 2) + n], at, keys))
                    at += keys
                return out, at

            def pe():
                def front(i):
                    if i >= 2:
                        nc.tensor.wait_ge(at_exp, b + i - 1)
                    for n, (products, keys) in enumerate(items[i]["scores"]):
                        mm = products(bank[4 * (i % 2) + n][:, 0:keys])
                    mm.then_inc(at_s, 1)

                def turn(i):
                    tiles = halves(i)[1] // P
                    nc.tensor.wait_ge(at_p, b + i + 1)
                    if i >= 2:
                        nc.tensor.wait_ge(at_oc, b + i - 1)
                        nc.tensor.wait_ge(at_pt, b + i - 1)
                    for j in range(tiles):
                        mm = nc.tensor.transpose(bank[4 * (i % 2) + 2 + j // 4][:, (j % 4) * P:(j % 4 + 1) * P],
                                                 row[i % 3][:, j * P:(j + 1) * P], ident)
                    mm.then_inc(at_t, 1)

                def values(i):
                    tiles = halves(i)[1] // P
                    nc.tensor.wait_ge(at_pt, b + i + 1)
                    o = bank[4 * (i % 2) + 3][items[i]["rows"], 2 * P:3 * P]
                    for j in range(tiles):
                        mm = nc.tensor.matmul(o, items[i]["v"](j), pt[i % 2][:, j, :], start=j == 0, stop=j == tiles - 1)
                    mm.then_inc(at_o, 1)

                front(0)
                for i in range(len(items) + 1):
                    if i + 1 < len(items):
                        front(i + 1)
                    if i < len(items):
                        turn(i)
                    if i:
                        values(i - 1)

            def act():
                def exps(i):
                    parts, total = halves(i)
                    nc.scalar.wait_ge(at_neg, b + i + 1)
                    m = MX[:, i % 2, :]
                    if items[i]["bias"] is None:
                        for n, (bk, a, keys) in enumerate(parts):
                            ins = nc.scalar.activation(row[i % 3][:, a:a + keys], bk[:, 0:keys], ACT.Exp, bias=m[:, 3:4],
                                                       scale=scale, accum_out=m[:, 4 + n:5 + n])
                    else:
                        ins = nc.scalar.activation(row[i % 3][:, 0:total], row[i % 3][:, 0:total], ACT.Exp, bias=m[:, 3:4],
                                                   scale=1.0, accum_out=m[:, 4:5])
                    ins.then_inc(at_exp, 1)

                def turned(i):
                    nc.scalar.wait_ge(at_t, b + i + 1)
                    tiles = halves(i)[1] // P
                    if i >= 2:
                        nc.scalar.wait_ge(at_o, b + i - 1)
                    lo = min(tiles, 4)
                    ins = nc.scalar.activation(pt[i % 2][:, 0:lo, :], bank[4 * (i % 2) + 2][:, 0:lo * P], ACT.Copy)
                    if tiles > 4:
                        ins = nc.scalar.activation(pt[i % 2][:, 4:tiles, :], bank[4 * (i % 2) + 3][:, 0:(tiles - 4) * P], ACT.Copy)
                    ins.then_inc(at_pt, 1)

                exps(0)
                for i in range(len(items)):
                    if i + 1 < len(items):
                        exps(i + 1)
                    turned(i)

            def dve():
                def maxima(i):
                    parts, total = halves(i)
                    m = MX[:, i % 2, :]
                    nc.vector.wait_ge(at_s, b + i + 1)
                    if i >= 3:
                        nc.vector.wait_ge(at_t, b + i - 2)
                    if items[i]["bias"] is None:
                        for n, (bk, a, keys) in enumerate(parts):
                            dv(nc.vector.tensor_reduce(m[:, n:n + 1], bk[:, 0:keys], AX.X, ALU.max))
                        dv.settle()
                        if len(parts) == 2:
                            dv.then(nc.vector.tensor_tensor(m[:, 0:1], m[:, 0:1], m[:, 1:2], ALU.max))
                        nc.vector.tensor_scalar(m[:, 3:4], m[:, 0:1], -scale, None, ALU.mult).then_inc(at_neg, 1)
                    else:
                        (b0, _, k0), (b1, a1, k1) = parts
                        nc.vector.wait_ge(*items[i]["bias_loaded"])
                        dv(nc.vector.scalar_tensor_tensor(row[i % 3][:, 0:k0], b0[:, 0:k0], scale, items[i]["bias"],
                                                          ALU.mult, ALU.add))
                        dv.then(nc.vector.tensor_scalar(row[i % 3][:, a1:a1 + k1], b1[:, 0:k1], scale, None, ALU.mult))
                        dv.then(nc.vector.tensor_reduce(m[:, 0:1], row[i % 3][:, 0:total], AX.X, ALU.max))
                        nc.vector.tensor_scalar(m[:, 3:4], m[:, 0:1], -1.0, None, ALU.mult).then_inc(at_neg, 1)

                def normed(i):
                    parts, total = halves(i)
                    m = MX[:, i % 2, :]
                    nc.vector.wait_ge(at_exp, b + i + 1)
                    if items[i]["bias"] is None and len(parts) == 2:
                        dv.then(nc.vector.tensor_tensor(m[:, 4:5], m[:, 4:5], m[:, 5:6], ALU.add))
                    dv.then(nc.vector.reciprocal(m[:, 6:7], m[:, 4:5]))
                    nc.vector.tensor_scalar(row[i % 3][:, 0:total], row[i % 3][:, 0:total], m[:, 6:7], None,
                                            ALU.mult).then_inc(at_p, 1)

                def out(i):
                    nc.vector.wait_ge(at_o, b + i + 1)
                    nc.vector.tensor_copy(items[i]["dst"], bank[4 * (i % 2) + 3][items[i]["rows"], 2 * P:3 * P]).then_inc(at_oc, 1)

                maxima(0)
                for i in range(len(items) + 2):
                    if i >= 2:
                        out(i - 2)
                    if i < len(items):
                        normed(i)
                    if i + 1 < len(items):
                        maxima(i + 1)

            phase(name, pe=pe, act=act, dve=dve, pool=pool)

        SMALL_ATT = SM(2, 8)

        def mla_attention():
            items = []
            for tl in range(NT):
                for h in range(H):
                    keys = [(0, S_CTX)] if tl < CT else [(0, 512), (512, TOK)]
                    rr = slice(ROPE * (h % 2), ROPE * (h % 2) + ROPE)
                    q = slice(tl * P, (tl + 1) * P)

                    def scores(bk, a, b_, h=h, rr=rr, q=q):
                        nc.tensor.matmul(bk, QN[:, h, q], KN[:, h, a:b_], start=True, stop=False)
                        return nc.tensor.matmul(bk, QR[rr, h // 2, q], KR[rr, a:b_], start=False, stop=True)
                    items.append(dict(
                        scores=[(lambda bk, a=a, b_=b_, f=scores: f(bk, a, b_), b_ - a) for a, b_ in keys],
                        bias=None, v=lambda j, h=h: VM[:, j, h * P:(h + 1) * P],
                        dst=MIXM[:, h, q], rows=slice(0, P)))
            attention("mla_attention", items, ROW, PT, MLA_SCALE)

        def keep_mla():
            def act():
                nc.scalar.dma_start(t["mla_mix"].rearrange("p (h n) -> p h n", h=H), MIXM).then_inc(stored, 16)
                nc.scalar.wait_ge(stored, 16)
            phase("keep_mla", act=act)

        QT, KT, VT = A(6144, H, TOK), A(9216, H, TOK), A(12288, H, TOK)
        GAP = S_CTX + 4
        RAW = [A(15360, TOK + 8), A(16136, TOK + 8)]
        CONV = [A(16912, TOK + 4), A(17684, TOK + 4)]
        SZ = A(18456, NT, HW)
        AB = A(21528, NT, 16)
        G, BETA, EG, EL, ET = (A(21624 + 48 * i, NT, 8) for i in range(5))
        KTOK, VTOK = A(0, NT, HW), A(3072, NT, HW)
        OG = A(12288, NT, HW)
        cv_full, cv_raw, cv_conv, cv_silu, cv_pad = (sem(f"cv_{x}") for x in ("full", "raw", "conv", "silu", "pad"))

        def gdn_qkv():
            UT = A(0, KB, TOK)
            idxs = [chunk(t["even_w_in"][:, j * CW:(j + 1) * CW], KB, CW) for j in range(3 * HW // CW)]
            nblk = 3 * H
            for j, idx in enumerate(idxs):
                released[idx] = (cv_full, 2 * j + 2)
            dest = [QT, KT, VT]

            def pe():
                for f in range(nblk):
                    if f % 2 == 0:
                        wait_chunk(nc.tensor, idxs[f // 2])
                    if f >= 2:
                        nc.tensor.wait_ge(cv_raw, f - 1)
                    for n, (a, b_) in enumerate(ALL):
                        for k in range(KB):
                            mm = nc.tensor.matmul(bank[2 * (f % 2) + n][:, 0:b_ - a],
                                                  slot(idxs[f // 2])[:, k, (f % 2) * P:(f % 2 + 1) * P],
                                                  UT[:, k, a:b_], start=k == 0, stop=k == KB - 1)
                    mm.then_inc(cv_full, 1)

            def pool():
                for r in RAW:
                    for a, b_ in ((0, 2), (S_CTX + 2, S_CTX + 6), (TOK + 6, TOK + 8)):
                        po(nc.gpsimd.memset(r[:, a:b_], 0.0))
                po.settle()
                nc.gpsimd.drain().then_inc(cv_pad, 1)

            def act():
                def raw(f):
                    nc.scalar.wait_ge(cv_full, f + 1)
                    if f >= 2:
                        nc.scalar.wait_ge(cv_conv, f - 1)
                    r, (b0, b1) = RAW[f % 2], bank[2 * (f % 2):2 * (f % 2) + 2]
                    nc.scalar.activation(r[:, 2:2 + S_CTX], b0[:, 0:S_CTX], ACT.Copy)
                    nc.scalar.activation(r[:, GAP + 2:GAP + 2 + 128], b0[:, S_CTX:384], ACT.Copy)
                    nc.scalar.activation(r[:, GAP + 130:GAP + 2 + S_LAT], b1[:, 0:384], ACT.Copy).then_inc(cv_raw, 1)

                def silu(f):
                    nc.scalar.wait_ge(cv_conv, f + 1)
                    c, d = CONV[f % 2], dest[f // H][:, f % H, :]
                    nc.scalar.activation(d[:, 0:S_CTX], c[:, 0:S_CTX], ACT.Silu)
                    nc.scalar.activation(d[:, S_CTX:TOK], c[:, GAP:GAP + S_LAT], ACT.Silu).then_inc(cv_silu, 1)

                for f in range(nblk + 1):
                    if f < nblk:
                        raw(f)
                    if f:
                        silu(f - 1)

            def dve():
                nc.vector.wait_ge(cv_pad, 1)
                for f in range(nblk):
                    nc.vector.wait_ge(cv_raw, f + 1)
                    if f >= 2:
                        nc.vector.wait_ge(cv_silu, f - 1)
                    r, c = RAW[f % 2], CONV[f % 2]
                    n = TOK + 4
                    dv.then(nc.vector.tensor_scalar(c, r[:, 0:n], CONVW[:, f, 0:1], None, ALU.mult))
                    for j in range(1, TAPS):
                        ins = nc.vector.scalar_tensor_tensor(c, r[:, j:j + n], CONVW[:, f, j:j + 1], c, ALU.mult, ALU.add)
                        if j < TAPS - 1:
                            dv.then(ins)
                        else:
                            ins.then_inc(cv_conv, 1)

            phase("gdn_qkv", pe=pe, act=act, dve=dve, pool=pool)

        def gdn_gate_inputs():
            w = t["even_w_in"]
            jobs = weights_to_tokens(w[:, 3 * HW:4 * HW], HW, lambda tl, a, b: SZ[:, tl, a:b], range(NT))
            jobs += weights_to_tokens(w[:, 4 * HW:4 * HW + 16], 16, lambda tl, a, b: AB[:, tl, a:b], range(NT))
            project("gdn_gates", jobs)

        nm_sq, nm_sum, nm_rs, nm_out = (sem(f"nm_{x}") for x in ("sq", "sum", "rs", "out"))
        dc_g = sem("dc_g")

        def gdn_norm():
            SQ = [A(21900, TOK), A(22668, TOK)]
            RN = [A(23436, TOK), A(24204, TOK)]
            TA, TB, TC, TD = (A(24972 + 48 * i, NT, 8) for i in range(4))
            blocks = [(x, h) for x in (QT, KT) for h in range(H)]

            def act():
                nc.scalar.activation(SZ, SZ, ACT.Silu)
                nc.scalar.wait_ge(dc_g, 1)
                nc.scalar.activation(TB, TB, ACT.Exp, scale=-1.0).then_inc(dc_g, 1)
                for i, (x, h) in enumerate(blocks):
                    if i >= 2:
                        nc.scalar.wait_ge(nm_sum, i - 1)
                    nc.scalar.activation(SQ[i % 2], x[:, h, :], ACT.Square).then_inc(nm_sq, 1)
                    if i:
                        rs(i - 1)
                rs(len(blocks) - 1)

            def rs(i):
                nc.scalar.wait_ge(nm_sum, i + 1)
                if i >= 2:
                    nc.scalar.wait_ge(nm_out, i - 1)
                for n, (a, b_) in enumerate(ALL):
                    ac(nc.scalar.activation(RN[i % 2][:, a:b_], bank[2 * (i % 2) + n][:, 0:b_ - a], ACT.Ln, bias=C("eps")))
                ac.settle()
                nc.scalar.activation(RN[i % 2], RN[i % 2], ACT.Exp, scale=-0.5,
                                     bias=C("ln_gdn_scale") if i < H else 0.0).then_inc(nm_rs, 1)

            def pe():
                for i in range(len(blocks)):
                    nc.tensor.wait_ge(nm_sq, i + 1)
                    if i >= 2:
                        nc.tensor.wait_ge(nm_rs, i - 1)
                    for n, (a, b_) in enumerate(ALL):
                        mm = nc.tensor.matmul(bank[2 * (i % 2) + n][:, 0:b_ - a], ones, SQ[i % 2][:, a:b_], start=True, stop=True)
                    mm.then_inc(nm_sum, 1)

            def dve():
                a, b_ = AB[:, :, 0:8], AB[:, :, 8:16]
                dt = DTB.rearrange("p (a c) -> p a c", a=1).to_broadcast([P, NT, 8])
                al = ALOG.rearrange("p (a c) -> p a c", a=1).to_broadcast([P, NT, 8])
                dv.then(nc.vector.tensor_tensor(a, a, dt, ALU.add))
                dv.then(nc.vector.tensor_scalar(TA, a, -1.0, None, ALU.mult))
                dv.then(nc.vector.tensor_tensor(TB, TA, a, ALU.max))
                dv.then(nc.vector.tensor_scalar(TA, a, 0.0, None, ALU.max))
                nc.vector.drain().then_inc(dc_g, 1)
                nc.vector.wait_ge(dc_g, 2)
                dv.then(nc.vector.tensor_scalar(TC, TB, 2.0, None, ALU.add))
                dv.then(nc.vector.reciprocal(TC, TC))
                dv.then(nc.vector.tensor_tensor(TB, TB, TC, ALU.mult))
                dv.then(nc.vector.tensor_tensor(TC, TB, TB, ALU.mult))
                dv.then(nc.vector.tensor_scalar(TD, TC, 1.0 / 19, None, ALU.mult))
                for odd in range(17, 1, -2):
                    dv.then(nc.vector.scalar_tensor_tensor(TD, TD, 1.0 / odd, TC, ALU.add, ALU.mult))
                dv.then(nc.vector.scalar_tensor_tensor(TB, TD, 1.0, TB, ALU.add, ALU.mult))
                dv.then(nc.vector.tensor_scalar(TB, TB, 2.0, None, ALU.mult))
                dv.then(nc.vector.tensor_tensor(TA, TA, TB, ALU.add))
                dv.then(nc.vector.scalar_tensor_tensor(G, TA, -1.0, al, ALU.mult, ALU.mult))
                nc.vector.drain().then_inc(dc_g, 1)
                for i, (x, h) in enumerate(blocks):
                    nc.vector.wait_ge(nm_rs, i + 1)
                    nc.vector.tensor_tensor(x[:, h, :], x[:, h, :], RN[i % 2], ALU.mult).then_inc(nm_out, 1)

            phase("gdn_norm", pe=pe, act=act, dve=dve)

        cum = {x: sem(f"cum_{x}") for x in ("rows", "sums", "cols", "col_copy", "last", "last_copy", "sum_exps")}
        BEG = SM(NT, 2 * H)
        GS, TOT1, TOT2, PAIR1, PAIR2 = (SM(NT, 2 * H) for _ in range(5))
        CHUNK, SUB = 64, 16

        def first_half(d):
            return C("level0_6")[:, P - 1:P] if d == 0 else C("level1_6")[:, 0:1]

        def gdn_cumsum():
            ROW = [A(25200, TOK)[0:H, :], A(25968, TOK)[0:H, :]]
            BT = [A(26736, 12, 4)[0:H], A(26784, 12, 4)[0:H]]
            E1, E2, E3 = A(26832, NT, 2 * H), A(26880, NT, 2 * H), A(26928, NT, 2 * H)
            groups = [(tl, d) for tl in range(NT) for d in range(2)]
            mod_pe, mod_act, mod_dve, _ = modulation(1, 0, MOD1_CUTS[0], (5, 6, 7), 27100)

            def pe():
                for d in range(2):
                    for tl in range(NT):
                        mm = nc.tensor.transpose(bank[2 * d + tl // 4][0:H, (tl % 4) * P:(tl % 4 + 1) * P],
                                                 G[:, tl, 4 * d:4 * d + 4], ident)
                    mm.then_inc(cum["rows"], 1)
                mod_pe()
                for d in range(2):
                    nc.tensor.wait_ge(cum["sums"], d + 1)
                    for tl in range(NT):
                        mm = nc.tensor.transpose(bank[4][:, 8 * tl + 4 * d:8 * tl + 4 * d + 4], ROW[d][:, tl * P:(tl + 1) * P],
                                                 ident[0:H, 0:H])
                mm.then_inc(cum["cols"], 1)
                nc.tensor.wait_ge(cum["col_copy"], 1)
                for i, (tl, d) in enumerate(groups):
                    if i >= 4:
                        nc.tensor.wait_ge(cum["last_copy"], i - 3)
                    mm = sums_at_queries(bank[i % 4], tl, d)
                    mm.then_inc(cum["last"], 1)

            def dve():
                def blocks(d):
                    return ROW[d].rearrange("p (c j) -> p c j", j=SUB)

                nc.vector.wait_ge(cum["rows"], 2)
                for d in range(2):
                    dv(nc.vector.tensor_copy(ROW[d][:, 0:512], bank[2 * d][0:H, :]))
                    dv(nc.vector.tensor_copy(ROW[d][:, 512:TOK], bank[2 * d + 1][0:H, 0:TOK - 512]))
                dv.settle()
                for j in range(1, SUB):
                    for d, (at, before) in enumerate(((j, j - 1), (SUB - 1 - j, SUB - j))):
                        b_ = blocks(d)
                        dv(nc.vector.tensor_tensor(b_[:, :, at:at + 1], b_[:, :, before:before + 1], b_[:, :, at:at + 1], ALU.add))
                    dv.settle()
                for d in range(2):
                    last = SUB - 1 if d == 0 else 0
                    dv(nc.vector.tensor_copy(BT[d].rearrange("p c b -> p (c b)").rearrange("p (c a) -> p c a", a=1),
                                             blocks(d)[:, :, last:last + 1]))
                dv.settle()
                for step in (1, 2):
                    for d in range(2):
                        k, before = (step, step - 1) if d == 0 else (3 - step, 4 - step)
                        dv(nc.vector.tensor_tensor(BT[d][:, :, k:k + 1], BT[d][:, :, before:before + 1], BT[d][:, :, k:k + 1], ALU.add))
                    dv.settle()
                for k in range(3):
                    for d in range(2):
                        src, dst = (k, k + 1) if d == 0 else (3 - k, 2 - k)
                        r = ROW[d].rearrange("p (c b j) -> p c b j", b=4, j=SUB)[:, :, dst, :]
                        dv(nc.vector.tensor_tensor(r, r, BT[d][:, :, src:src + 1].to_broadcast([H, 12, SUB]), ALU.add))
                dv.settle()
                nc.vector.drain().then_inc(cum["sums"], 2)
                nc.vector.wait_ge(cum["cols"], 1)
                nc.vector.tensor_copy(GS, bank[4][:, 0:48].rearrange("p (t g) -> p t g", t=NT)).then_inc(cum["col_copy"], 1)
                for i, (tl, d) in enumerate(groups):
                    nc.vector.wait_ge(cum["last"], i + 1)
                    b_ = heads(bank[i % 4][:, :])
                    at1, at2 = (CHUNK - 1, P - 1) if d == 0 else (CHUNK, 0)
                    cols = slice(4 * d, 4 * d + 4)
                    dv(nc.vector.tensor_copy(TOT1[:, tl, cols].rearrange("p (h a) -> p h a", a=1), b_[:, :, at1:at1 + 1]))
                    nc.vector.tensor_copy(TOT2[:, tl, cols].rearrange("p (h a) -> p h a", a=1),
                                          b_[:, :, at2:at2 + 1]).then_inc(cum["last_copy"], 1)
                dv.settle()
                nc.vector.wait_ge(cum["last_copy"], len(groups))
                dv(nc.vector.tensor_scalar(PAIR1, GS, -1.0, None, ALU.mult))
                dv(nc.vector.tensor_tensor(E3, TOT1, TOT2, ALU.add))
                for d in range(2):
                    cols = slice(4 * d, 4 * d + 4)
                    dv(nc.vector.tensor_scalar(E1[:, :, cols], TOT1[:, :, cols], first_half(1 - d), None, ALU.mult))
                    dv(nc.vector.tensor_scalar(E2[:, :, cols], TOT1[:, :, cols], first_half(d), None, ALU.mult))
                dv.settle()
                dv(nc.vector.tensor_tensor(E1, E1, GS, ALU.add))
                dv.then(nc.vector.tensor_tensor(PAIR2, E2, GS, ALU.subtract))
                dv(nc.vector.tensor_tensor(E2, PAIR2, TOT2, ALU.add))
                dv.settle()
                nc.vector.drain().then_inc(cum["sum_exps"], 1)
                mod_dve()

            def act():
                nc.scalar.activation(BETA, AB[:, :, 8:16], ACT.Sigmoid)
                mod_act()
                nc.scalar.wait_ge(cum["sum_exps"], 1)
                for dst, src in ((EG, E1), (EL, E2), (ET, E3)):
                    nc.scalar.activation(dst, src, ACT.Exp)

            phase("gdn_cumsum", pe=pe, act=act, dve=dve)

        def sums_at_queries(bk, tl, d):
            for h in range(H):
                mm = nc.tensor.transpose(heads(bk[:, :])[:, h, :], GS[:, tl, 4 * d + h:4 * d + h + 1].to_broadcast([P, P]), ident)
            return mm

        tk_full, tk_done = sem("tk_full"), sem("tk_done")

        def gdn_tokens():
            items = [(x, y, tl) for x, y in ((KT, KTOK), (VT, VTOK)) for tl in range(NT)]

            def pe():
                for i, (x, y, tl) in enumerate(items):
                    if i >= 4:
                        nc.tensor.wait_ge(tk_done, i - 3)
                    for h in range(H):
                        mm = nc.tensor.transpose(bank[i % 4][:, h * P:(h + 1) * P], x[:, h, tl * P:(tl + 1) * P], ident)
                    mm.then_inc(tk_full, 1)

            def act():
                for i, (x, y, tl) in enumerate(items):
                    nc.scalar.wait_ge(tk_full, i + 1)
                    nc.scalar.activation(y[:, tl, :], bank[i % 4][:, :], ACT.Copy).then_inc(tk_done, 1)

            def dve():
                nc.vector.tensor_tensor(BEG, BETA, EG, ALU.mult)
            phase("gdn_tokens", pe=pe, act=act, dve=dve)

        def bufs(*at):
            return [A(a, H, P) for a in at]

        gd = {x: sem(f"gd_{x}") for x in (
            "in", "dec", "kbt", "diff", "exps", "pair", "qe", "attn", "qkd", "bt", "tt", "t", "turn", "u", "ucopy", "upd", "tnew",
            "rhs", "sol", "solcopy", "ws", "vnew", "out", "done", "zero")}

        def gdn_scan():
            groups = [(n, d) for n in range(NT) for d in range(2)]
            B = [bufs(*range(15360, 15360 + 6 * 512, 512), *range(21900, 21900 + 2 * 512, 512)),
                 bufs(*range(22924, 22924 + 8 * 512, 512))]
            S = bufs(27020, 27532)
            AT = KL = [b[0] for b in B]
            KBB = BTA = VB = [b[1] for b in B]
            ETM = BTB = KBE = [b[2] for b in B]
            QE = [b[3] for b in B]
            KBT = TT = [b[4] for b in B]
            T_ = WT = [b[5] for b in B]
            U = VN = [b[6] for b in B]
            QK = [b[7] for b in B]

            def tile(n, d):
                tl = ORDER[d][n]
                return tl, slice(tl * P, (tl + 1) * P)

            def gcol(x, d, tl):
                return over_cols(x[:, tl, 4 * d:4 * d + 4])

            def bk(d, i):
                return bank[4 * d + i]

            def each_head(out, lhs, rhs, start=True, stop=True):
                for h in range(H):
                    mm = nc.tensor.matmul(heads(out[:, :])[:, h, :], lhs(h), rhs(h), start=start, stop=stop)
                return mm

            def pe():
                for n in range(NT):
                    for d in range(2):
                        g = 2 * n + d
                        nc.tensor.wait_ge(gd["in"], g + 1)
                        if n:
                            nc.tensor.wait_ge(gd["done"], g - 1)
                        sums_at_queries(bk(d, 0), tile(n, d)[0], d)
                        for h in range(H):
                            mm = nc.tensor.transpose(heads(bk(d, 2)[:, :])[:, h, :], KBB[d][:, h, :], ident)
                        mm.then_inc(gd["dec"], 1)
                    for d in range(2):
                        g = 2 * n + d
                        tl, cols = tile(n, d)
                        nc.tensor.wait_ge(gd["kbt"], g + 1)
                        each_head(bk(d, 3), lambda h: KT[:, h, cols], lambda h: KBT[d][:, h, :])
                        each_head(bk(d, 1), lambda h: KT[:, h, cols], lambda h: QT[:, h, cols]).then_inc(gd["pair"], 1)
                    for d in range(2):
                        g = 2 * n + d
                        nc.tensor.wait_ge(gd["tt"], g + 1)
                        nc.tensor.wait_ge(gd["qkd"], g + 1)
                        for h in range(H):
                            mm = nc.tensor.transpose(heads(bk(d, 1)[:, :])[:, h, :], TT[d][:, h, :], ident)
                        mm.then_inc(gd["turn"], 1)
                    for l in range(1, LEVELS):
                        for d in range(2):
                            g, m = 2 * n + d, (2 * n + d) * (LEVELS - 1) + l
                            BT = (BTA, BTB)[l % 2][d]
                            nc.tensor.wait_ge(gd["bt"], (2 * n * LEVELS) + 2 * l + d + 1)
                            if l == 1:
                                nc.tensor.wait_ge(gd["t"], g + 1)
                            else:
                                nc.tensor.wait_ge(gd["tnew"], 2 * n * (LEVELS - 1) + 2 * (l - 2) + d + 1)
                            each_head(bk(d, 1), lambda h: BT[:, h, :], lambda h: T_[d][:, h, :]).then_inc(gd["u"], 1)
                        for d in range(2):
                            nc.tensor.wait_ge(gd["ucopy"], 2 * n * (LEVELS - 1) + 2 * (l - 1) + d + 1)
                            if l < LEVELS - 1:
                                each_head(bk(d, 2), lambda h: TT[d][:, h, :], lambda h: U[d][:, h, :])
                            each_head(bk(d, 3), lambda h: U[d][:, h, :], lambda h: TT[d][:, h, :]).then_inc(gd["upd"], 1)
                    for d in range(2):
                        g = 2 * n + d
                        nc.tensor.wait_ge(gd["rhs"], g + 1)
                        nc.tensor.wait_ge(gd["tnew"], (2 * n * (LEVELS - 1)) + 2 * (LEVELS - 2) + d + 1)
                        each_head(bk(d, 1), lambda h: TT[d][:, h, :], lambda h: VB[d][:, h, :])
                        each_head(bk(d, 2), lambda h: KBE[d][:, h, :], lambda h: TT[d][:, h, :]).then_inc(gd["sol"], 1)
                    for d in range(2):
                        g = 2 * n + d
                        nc.tensor.wait_ge(gd["solcopy"], g + 1)
                        if n == 0 and d == 0:
                            nc.tensor.wait_ge(gd["zero"], 1)
                        each_head(bk(d, 3), lambda h: WT[d][:, h, :], lambda h: S[d][:, h, :]).then_inc(gd["ws"], 1)
                    for d in range(2):
                        g = 2 * n + d
                        nc.tensor.wait_ge(gd["vnew"], g + 1)
                        nc.tensor.wait_ge(gd["qe"], g + 1)
                        for h in range(H):
                            o = heads(bk(d, 0)[:, :])[:, h, :]
                            nc.tensor.matmul(o, QE[d][:, h, :], S[d][:, h, :], start=True, stop=False)
                            nc.tensor.matmul(o, QK[d][:, h, :], VN[d][:, h, :], start=False, stop=True)
                        each_head(bk(d, 1), lambda h: KL[d][:, h, :], lambda h: VN[d][:, h, :]).then_inc(gd["out"], 1)

            def act():
                for n in range(NT):
                    for d in range(2):
                        g = 2 * n + d
                        nc.scalar.wait_ge(gd["dec"], g + 1)
                        nc.scalar.activation(KBT[d], heads(bk(d, 2)[:, :]), ACT.Copy).then_inc(gd["kbt"], 1)
                    for d in range(2):
                        nc.scalar.wait_ge(gd["diff"], 2 * n + d + 1)
                        nc.scalar.activation(QE[d], QE[d], ACT.Exp)
                        nc.scalar.activation(ETM[d], ETM[d], ACT.Exp).then_inc(gd["exps"], 1)
                    for d in range(2):
                        g = 2 * n + d
                        nc.scalar.wait_ge(gd["turn"], g + 1)
                        nc.scalar.activation(T_[d], heads(bk(d, 1)[:, :]), ACT.Copy).then_inc(gd["t"], 1)
                    for l in range(1, LEVELS):
                        for d in range(2):
                            nc.scalar.wait_ge(gd["u"], 2 * n * (LEVELS - 1) + 2 * (l - 1) + d + 1)
                            nc.scalar.activation(U[d], heads(bk(d, 1)[:, :]), ACT.Copy).then_inc(gd["ucopy"], 1)
                    for d in range(2):
                        g = 2 * n + d
                        nc.scalar.wait_ge(gd["sol"], g + 1)
                        nc.scalar.activation(U[d], heads(bk(d, 1)[:, :]), ACT.Copy)
                        nc.scalar.activation(WT[d], heads(bk(d, 2)[:, :]), ACT.Copy).then_inc(gd["solcopy"], 1)

            def pool():
                for d in range(2):
                    po(nc.gpsimd.memset(S[d], 0.0))
                po(nc.gpsimd.memset(OG, 0.0))
                po.settle()
                nc.gpsimd.drain().then_inc(gd["zero"], 1)
                for n in range(NT):
                    for d in range(2):
                        g = 2 * n + d
                        tl, cols = tile(n, d)
                        if n:
                            nc.gpsimd.wait_ge(gd["done"], g - 1)
                        nc.gpsimd.tensor_tensor(KBB[d], heads(KTOK[:, tl, :]), gcol(BETA, d, tl), ALU.mult).then_inc(gd["in"], 1)
                    for d in range(2):
                        nc.gpsimd.wait_ge(gd["exps"], 2 * n + d + 1)
                        nc.gpsimd.tensor_tensor(QE[d], QE[d], QT[:, :, tile(n, d)[1]], ALU.mult).then_inc(gd["qe"], 1)
                    for l in range(LEVELS):
                        for d in range(2):
                            g = 2 * n + d
                            if l == 0:
                                nc.gpsimd.wait_ge(gd["attn"], g + 1)
                            if l == 1:
                                nc.gpsimd.wait_ge(gd["qkd"], g + 1)
                            if l >= 2:
                                if l == 2:
                                    nc.gpsimd.wait_ge(gd["tt"], g + 1)
                                else:
                                    nc.gpsimd.wait_ge(gd["u"], 2 * n * (LEVELS - 1) + 2 * (l - 3) + d + 1)
                            nc.gpsimd.tensor_tensor((BTA, BTB)[l % 2][d], AT[d], over_heads(C(f"level{d}_{l}")),
                                                    ALU.mult).then_inc(gd["bt"], 1)
                    for d in range(2):
                        g = 2 * n + d
                        tl, cols = tile(n, d)
                        nc.gpsimd.wait_ge(gd["bt"], 2 * (n + 1) * LEVELS)
                        po(nc.gpsimd.tensor_tensor(KL[d], heads(KTOK[:, tl, :]), gcol(EL, d, tl), ALU.mult))
                    for d in range(2):
                        tl, cols = tile(n, d)
                        nc.gpsimd.wait_ge(gd["u"], 2 * n * (LEVELS - 1) + 2 * (LEVELS - 3) + d + 1)
                        po(nc.gpsimd.tensor_tensor(KBE[d], heads(KTOK[:, tl, :]), gcol(BEG, d, tl), ALU.mult))
                    po.settle()
                    for d in range(2):
                        tl, cols = tile(n, d)
                        nc.gpsimd.wait_ge(gd["u"], 2 * n * (LEVELS - 1) + 2 * (LEVELS - 2) + d + 1)
                        nc.gpsimd.tensor_tensor(VB[d], heads(VTOK[:, tl, :]), gcol(BETA, d, tl), ALU.mult).then_inc(gd["rhs"], 1)

            def dve():
                for n in range(NT):
                    for d in range(2):
                        g = 2 * n + d
                        tl, cols = tile(n, d)
                        halves = (slice(0, CHUNK), slice(CHUNK, P)) if d == 0 else (slice(CHUNK, P), slice(0, CHUNK))
                        sums = heads(bk(d, 0)[:, :])
                        scal = lambda x: over_cols(x[:, tl, 4 * d:4 * d + 4], CHUNK)
                        nc.vector.wait_ge(gd["dec"], g + 1)
                        dv(nc.vector.tensor_tensor(ETM[d][:, :, halves[0]], sums[:, :, halves[0]], scal(PAIR1), ALU.add))
                        dv(nc.vector.tensor_tensor(ETM[d][:, :, halves[1]], sums[:, :, halves[1]], scal(PAIR2), ALU.add))
                        dv(nc.vector.tensor_copy(QE[d][:, :, halves[0]], sums[:, :, halves[0]]))
                        dv.then(nc.vector.tensor_tensor(QE[d][:, :, halves[1]], sums[:, :, halves[1]], scal(TOT1), ALU.add))
                        nc.vector.tensor_scalar(ETM[d], ETM[d], 0.0, None, ALU.min).then_inc(gd["diff"], 1)
                    for d in range(2):
                        g = 2 * n + d
                        tl, cols = tile(n, d)
                        nc.vector.wait_ge(gd["exps"], g + 1)
                        dv(nc.vector.tensor_tensor(ETM[d], ETM[d], over_heads(C(f"incl{d}")), ALU.mult))
                    for d in range(2):
                        g = 2 * n + d
                        nc.vector.wait_ge(gd["pair"], g + 1)
                        dv.settle()
                        nc.vector.tensor_tensor(AT[d], heads(bk(d, 3)[:, :]), ETM[d], ALU.mult).then_inc(gd["attn"], 1)
                        nc.vector.tensor_tensor(QK[d], heads(bk(d, 1)[:, :]), ETM[d], ALU.mult).then_inc(gd["qkd"], 1)
                    for d in range(2):
                        g = 2 * n + d
                        nc.vector.wait_ge(gd["bt"], 2 * n * LEVELS + d + 1)
                        nc.vector.tensor_tensor(TT[d], over_heads(ident), BTA[d], ALU.subtract).then_inc(gd["tt"], 1)
                    for l in range(1, LEVELS):
                        for d in range(2):
                            nc.vector.wait_ge(gd["upd"], 2 * n * (LEVELS - 1) + 2 * (l - 1) + d + 1)
                            if l < LEVELS - 1:
                                if l == 1:
                                    nc.vector.wait_ge(gd["t"], 2 * n + d + 1)
                                dv(nc.vector.tensor_tensor(T_[d], T_[d], heads(bk(d, 2)[:, :]), ALU.subtract))
                                dv.settle()
                            nc.vector.tensor_tensor(TT[d], TT[d], heads(bk(d, 3)[:, :]), ALU.subtract).then_inc(gd["tnew"], 1)
                    for d in range(2):
                        g = 2 * n + d
                        nc.vector.wait_ge(gd["ws"], g + 1)
                        nc.vector.tensor_tensor(VN[d], U[d], heads(bk(d, 3)[:, :]), ALU.subtract).then_inc(gd["vnew"], 1)
                    if n == 0:
                        nc.vector.wait_ge(gd["zero"], 1)
                    for d in range(2):
                        g = 2 * n + d
                        tl, cols = tile(n, d)
                        nc.vector.wait_ge(gd["out"], g + 1)
                        dv(nc.vector.tensor_tensor(OG[:, tl, :], OG[:, tl, :], bk(d, 0)[:, :], ALU.add))
                        dv.then(nc.vector.tensor_tensor(S[d], S[d], gcol(ET, d, tl), ALU.mult))
                        nc.vector.tensor_tensor(S[d], S[d], heads(bk(d, 1)[:, :]), ALU.add).then_inc(gd["done"], 1)

            phase("gdn_scan", pe=pe, act=act, dve=dve, pool=pool)

        gt_sq, gt_rs, gt_ready, gt_full, gt_done = (sem(f"gt_{x}") for x in ("sq", "rs", "ready", "full", "done"))

        def gated_norm(l, O, Z, SQ, MIX, tiles):
            nt = len(tiles)
            b, bt = base("gt", 1), base("gtt", nt)
            R = STAT.rearrange("p a b -> p (a b)")[:, 0:4 * nt]
            R3 = R.rearrange("p (t h) -> p t h", t=nt)

            def act():
                nc.scalar.activation(SQ, O, ACT.Square).then_inc(gt_sq, 1)
                nc.scalar.wait_ge(gt_rs, 2 * b + 1)
                ac.then(nc.scalar.activation(R, R, ACT.Ln, bias=C("eps"), scale=1.0 / P))
                nc.scalar.activation(R, R, ACT.Exp, scale=-0.5).then_inc(gt_rs, 1)
                for i in range(nt):
                    nc.scalar.wait_ge(gt_full, bt + i + 1)
                    nc.scalar.activation(MIX[:, :, i * P:(i + 1) * P], heads(bank[i % 4][:, :]), ACT.Copy).then_inc(gt_done, 1)

            def dve():
                nc.vector.wait_ge(gt_sq, b + 1)
                nc.vector.tensor_reduce(R, SQ.rearrange("p t (h c) -> p (t h) c", h=H), AX.X, ALU.add).then_inc(gt_rs, 1)
                nc.vector.wait_ge(gt_rs, 2 * b + 2)
                for i in range(nt):
                    o = heads(O[:, i, :])
                    dv.then(nc.vector.tensor_tensor(o, o, over_cols(R3[:, i, :]), ALU.mult))
                    dv.then(nc.vector.tensor_tensor(o, o, over_heads(GN[:, l, :]), ALU.mult))
                    nc.vector.tensor_tensor(O[:, i, :], O[:, i, :], Z[:, i, :], ALU.mult).then_inc(gt_ready, 1)

            def pe():
                for i in range(nt):
                    nc.tensor.wait_ge(gt_ready, bt + i + 1)
                    if i >= 4:
                        nc.tensor.wait_ge(gt_done, bt + i - 3)
                    for h in range(H):
                        mm = nc.tensor.transpose(bank[i % 4][:, h * P:(h + 1) * P], O[:, i, h * P:(h + 1) * P], ident)
                    mm.then_inc(gt_full, 1)

            phase(f"gated_norm{l}", pe=pe, act=act, dve=dve)

        NQ, NK, NV = A(6144, H, S_LAT), A(8192, H, TOK), A(11264, NT, HW)
        MIXN = A(14336, H, S_LAT)
        TZ = [A(16384, 16 * GRID), A(17408, 16 * GRID)]
        NROW = [A(18432, TOK), A(19200, TOK), A(21504, TOK)]
        NPT = [A(19968, NT, P), A(20736, NT, P)]

        def na_projections():
            w = t["odd_w_in"]
            jobs = weights_to_features(w[:, 0:HW], HW, lambda f, a, b: NQ[:, f, a - S_CTX:b - S_CTX], LAT)
            jobs += weights_to_features(w[:, HW:2 * HW], HW, lambda f, a, b: NK[:, f, a:b], ALL)
            jobs += weights_to_tokens(w[:, 2 * HW:3 * HW], HW, lambda tl, a, b: NV[:, tl, a:b], range(NT))
            project("na_projections", jobs)

        def na_attention():
            items = []
            for h in range(NA_H):
                for i in range(LT):
                    rr = slice(NA_D * (h % 2), NA_D * (h % 2) + NA_D)
                    q = slice(i * P, (i + 1) * P)
                    off = NA_KH - 1 - 2 * i

                    def scores(bk, a, b_, h=h, rr=rr, q=q):
                        return nc.tensor.matmul(bk, NQ[rr, h // 2, q], NK[rr, h // 2, a:b_], start=True, stop=True)
                    items.append(dict(
                        scores=[(lambda bk, f=scores: f(bk, S_CTX, TOK), S_LAT), (lambda bk, f=scores: f(bk, 0, S_CTX), S_CTX)],
                        bias=TZ[h % 2][:, off * GRID:(off + ROWS) * GRID], bias_loaded=(bias_in[h % 2], 16 * (h // 2 + 1)),
                        v=lambda j, h=h: NV[:, (CT + j) % NT, h * NA_D:(h + 1) * NA_D],
                        dst=MIXN[rr, h // 2, q], rows=rr))
            n_at = calls["at"]

            def pool():
                for h in range(NA_H):
                    if h >= 2:
                        nc.gpsimd.wait_ge(at_neg, n_at + LT * (h - 1))
                    nc.gpsimd.dma_start(TZ[h % 2], t["rpb_tables"][:, h, :]).then_inc(bias_in[h % 2], 16)

            attention("na_attention", items, NROW, NPT, NA_SCALE, pool=pool)

        HQ, ZT = A(6144, H, S_LAT), A(16384, 2, H * TOK)
        HV, SG = A(22528, NT, HW), A(25600, LT, HW)
        OH = A(8192, LT, HW)

        def hgrn_projections():
            w = t["odd_w_in"][:, 3 * HW:]
            jobs = weights_to_features(w[:, 0:HW], HW, lambda f, a, b: HQ[:, f, a - S_CTX:b - S_CTX], LAT)
            for d in range(2):
                z = ZT[:, d, :].rearrange("p (h n) -> p h n", h=H)
                jobs += weights_to_features(w[:, (1 + d) * HW:(2 + d) * HW], HW, lambda f, a, b, z=z: z[:, f, a:b], ALL)
            jobs += weights_to_tokens(w[:, 3 * HW:4 * HW], HW, lambda tl, a, b: HV[:, tl, a:b], range(NT))
            jobs += weights_to_tokens(w[:, 4 * HW:5 * HW], HW, lambda tl, a, b: SG[:, tl - CT, a:b], range(CT, NT))
            project("hgrn_projections", jobs)

            def act():
                nc.scalar.activation(HQ, HQ, ACT.Silu)
                nc.scalar.activation(SG, SG, ACT.Silu)
            phase("hgrn_silu", act=act)

        hg = {x: sem(f"hg_{x}") for x in (
            "sig", "cr", "qk", "att", "att_used", "fin", "qfin", "turn", "turncopy", "out", "done", "zero")}

        def hgrn_scan():
            B = [bufs(*range(0, 3584, 512)), bufs(*range(3584, 6144, 512), 10240, 10752)]
            S = bufs(11264, 11776)
            CC_, KS, R_, QC, KC, AT, KRT = ([b[i] for b in B] for i in range(7))

            def tile(n, d):
                tl = ORDER[d][n]
                return tl, slice(tl * P, (tl + 1) * P), slice((tl - CT) * P, (tl - CT + 1) * P)

            def bk(d, i):
                return bank[4 * d + i]

            def z(d, cols):
                return ZT[:, d, :].rearrange("p (h n) -> p h n", h=H)[:, :, cols]

            def is_lat(n):
                return n >= CT

            def split(x, l):
                return x.rearrange("p h (b s w) -> p (h b) s w", s=2, w=1 << l)

            NL = LEVELS + 1

            def at_level(n, l, d):
                return 2 * (n - CT) * NL + 2 * l + d + 1

            def each_head(out, lhs, rhs, start=True, stop=True):
                for h in range(H):
                    mm = nc.tensor.matmul(heads(out[:, :])[:, h, :], lhs(h), rhs(h), start=start, stop=stop)
                return mm

            def pe():
                for n in range(NT):
                    if is_lat(n):
                        for l in range(NL):
                            for d in range(2):
                                tl, cols, lat = tile(n, d)
                                out = bk(d, l % 2)
                                if l == 0:
                                    nc.tensor.wait_ge(hg["sig"], 2 * n + d + 1)
                                else:
                                    nc.tensor.wait_ge(hg["qk"], 2 * (2 * (n - CT) * LEVELS + 2 * (l - 1) + d + 1))
                                if l >= 2:
                                    nc.tensor.wait_ge(hg["att"], at_level(n, l - 2, d))
                                elif n > CT:
                                    nc.tensor.wait_ge(hg["done"], 2 * n + d - 1)
                                if l == 0:
                                    mm = each_head(out, lambda h: KS[d][:, h, :], lambda h: HQ[:, h, lat])
                                else:
                                    mm = each_head(out, lambda h: KC[d][:, h, :], lambda h: QC[d][:, h, :])
                                mm.then_inc(hg["att_used"], 1)
                    for d in range(2):
                        tl, cols, lat = tile(n, d)
                        nc.tensor.wait_ge(hg["fin"], 2 * n + d + 1)
                        for h in range(H):
                            mm = nc.tensor.transpose(heads(bk(d, 2)[:, :])[:, h, :], KC[d][:, h, :], ident)
                        mm.then_inc(hg["turn"], 1)
                    for d in range(2):
                        tl, cols, lat = tile(n, d)
                        g = 2 * n + d
                        nc.tensor.wait_ge(hg["turncopy"], g + 1)
                        if n == 0 and d == 0:
                            nc.tensor.wait_ge(hg["zero"], 1)
                        if is_lat(n):
                            nc.tensor.wait_ge(hg["att"], at_level(n, NL - 1, d))
                            nc.tensor.wait_ge(hg["qfin"], 2 * (n - CT) + d + 1)
                            if n:
                                nc.tensor.wait_ge(hg["done"], g - 1)
                            for h in range(H):
                                o = heads(bk(d, 0)[:, :])[:, h, :]
                                nc.tensor.matmul(o, QC[d][:, h, :], S[d][:, h, :], start=True, stop=False)
                                nc.tensor.matmul(o, AT[d][:, h, :], heads(HV[:, tl, :])[:, h, :], start=False, stop=True)
                        elif n:
                            nc.tensor.wait_ge(hg["done"], g - 1)
                        each_head(bk(d, 3), lambda h: KRT[d][:, h, :], lambda h: heads(HV[:, tl, :])[:, h, :]).then_inc(hg["out"], 1)

            def act():
                for n in range(NT):
                    for d in range(2):
                        tl, cols, lat = tile(n, d)
                        if n:
                            nc.scalar.wait_ge(hg["done"], 2 * n + d - 1)
                        ac(nc.scalar.activation(CC_[d], z(d, cols), ACT.Sigmoid))
                        ac(nc.scalar.activation(KS[d], z(d, cols), ACT.Sigmoid, scale=-1.0))
                        ac.settle()
                        for h in range(H):
                            nc.scalar.activation(CC_[d][:, h, :], CC_[d][:, h, :], ACT.Identity,
                                                 bias=LB[:, 4 * d + h:4 * d + h + 1], scale=OML[:, 4 * d + h:4 * d + h + 1])
                            ins = nc.scalar.activation(KS[d][:, h, :], KS[d][:, h, :], ACT.Copy,
                                                       scale=OML[:, 4 * d + h:4 * d + h + 1])
                        ins.then_inc(hg["sig"], 1)
                    for d in range(2):
                        nc.scalar.wait_ge(hg["turn"], 2 * n + d + 1)
                        nc.scalar.activation(KRT[d], heads(bk(d, 2)[:, :]), ACT.Copy).then_inc(hg["turncopy"], 1)

            def pool():
                for d in range(2):
                    po(nc.gpsimd.memset(S[d], 0.0))
                po.then(nc.gpsimd.memset(OH, 0.0))
                nc.gpsimd.drain().then_inc(hg["zero"], 1)
                for n in range(NT):
                    for l in range(LEVELS if is_lat(n) else 0):
                        for d in range(2):
                            tl, cols, lat = tile(n, d)
                            nc.gpsimd.wait_ge(hg["sig"], 2 * n + d + 1)
                            if l:
                                nc.gpsimd.wait_ge(hg["cr"], (2 * n * LEVELS) + 2 * (l - 1) + d + 1)
                                nc.gpsimd.wait_ge(hg["att_used"], at_level(n, l, d))
                                ks, r, kc = (split(x, l)[:, :, (0, 1)[d], :] for x in (KS[d], R_[d], KC[d]))
                                nc.gpsimd.tensor_tensor(kc, ks, r, ALU.mult).then_inc(hg["qk"], 1)
                                c, qc = (split(x, l)[:, :, (1, 0)[d], :] for x in (CC_[d], QC[d]))
                                q = HQ[:, :, lat].rearrange("p h (b s w) -> p h b s w", s=2, w=1 << l)[:, :, :, (1, 0)[d], :]
                                c, qc = (x.rearrange("p (h b) w -> p h b w", h=H) for x in (c, qc))
                                nc.gpsimd.tensor_tensor(qc, q, c, ALU.mult).then_inc(hg["qk"], 1)
                            else:
                                nc.gpsimd.tensor_copy(KC[d], KS[d]).then_inc(hg["qk"], 1)
                                nc.gpsimd.tensor_tensor(QC[d], HQ[:, :, lat], CC_[d], ALU.mult).then_inc(hg["qk"], 1)
                    for d in range(2):
                        tl, cols, lat = tile(n, d)
                        nc.gpsimd.wait_ge(hg["cr"], (2 * n * LEVELS) + 2 * (LEVELS - 1) + d + 1)
                        if is_lat(n):
                            nc.gpsimd.wait_ge(hg["att_used"], at_level(n, NL - 1, d))
                        elif n:
                            nc.gpsimd.wait_ge(hg["turn"], 2 * n + d - 1)
                        nc.gpsimd.tensor_tensor(KC[d], KS[d], R_[d], ALU.mult).then_inc(hg["fin"], 1)
                        if is_lat(n):
                            nc.gpsimd.tensor_tensor(QC[d], HQ[:, :, lat], CC_[d], ALU.mult).then_inc(hg["qfin"], 1)

            def grow(n, d, l):
                h2 = 1 << l
                c = CC_[d].rearrange("p h (b s w) -> p (h b) s w", s=2, w=h2)
                r = R_[d].rearrange("p h (b s w) -> p (h b) s w", s=2, w=h2)
                q, k = (1, 0) if d == 0 else (0, 1)
                near = h2 - 1 if d == 0 else 0
                nb = c.shape[1]
                full = [c[:, :, s, near:near + 1].to_broadcast([P, nb, h2]) for s in range(2)]
                if l == 0:
                    dv(nc.vector.memset(R_[d][:, :, :], 1.0))
                    dv.settle()
                dv.then(nc.vector.tensor_tensor(r[:, :, k, :], r[:, :, k, :], full[q], ALU.mult))
                nc.vector.tensor_tensor(c[:, :, q, :], c[:, :, q, :], full[k], ALU.mult).then_inc(hg["cr"], 1)

            def dve():
                nc.vector.wait_ge(hg["zero"], 1)
                for n in range(NT):
                    if not is_lat(n):
                        for l in range(LEVELS):
                            for d in range(2):
                                nc.vector.wait_ge(hg["sig"], 2 * n + d + 1)
                                if l:
                                    nc.vector.wait_ge(hg["cr"], 2 * n * LEVELS + 2 * (l - 1) + d + 1)
                                grow(n, d, l)
                    else:
                        for l in range(NL):
                            for d in range(2):
                                nc.vector.wait_ge(hg["att_used"], at_level(n, l, d))
                                b_ = heads(bk(d, l % 2)[:, :])
                                if l == 0:
                                    ins = nc.vector.tensor_tensor(AT[d], b_, over_heads(ident), ALU.mult)
                                else:
                                    mask = over_heads(C(f"level{d}_{l - 1}").bitcast(I32))
                                    ins = nc.vector.copy_predicated(AT[d], mask, b_)
                                ins.then_inc(hg["att"], 1)
                                if l < LEVELS:
                                    nc.vector.wait_ge(hg["qk"], 2 * (2 * (n - CT) * LEVELS + 2 * l + d + 1))
                                    if l:
                                        nc.vector.wait_ge(hg["cr"], 2 * n * LEVELS + 2 * (l - 1) + d + 1)
                                    grow(n, d, l)
                                nc.vector.wait_ge(hg["att"], at_level(n, l, d))
                    for d in range(2):
                        g = 2 * n + d
                        tl, cols, lat = tile(n, d)
                        last = P - 1 if d == 0 else 0
                        nc.vector.wait_ge(hg["out"], g + 1)
                        nc.vector.wait_ge(hg["cr"], 2 * n * LEVELS + 2 * (LEVELS - 1) + d + 1)
                        if is_lat(n):
                            dv(nc.vector.tensor_tensor(OH[:, tl - CT, :], OH[:, tl - CT, :], bk(d, 0)[:, :], ALU.add))
                        total = CC_[d][:, :, last:last + 1].to_broadcast([P, H, P])
                        dv.then(nc.vector.tensor_tensor(S[d], S[d], total, ALU.mult))
                        nc.vector.tensor_tensor(S[d], S[d], heads(bk(d, 3)[:, :]), ALU.add).then_inc(hg["done"], 1)
                        nc.vector.wait_ge(hg["done"], g + 1)

            phase("hgrn_scan", pe=pe, act=act, dve=dve, pool=pool)

        OSC = A(16384, NT, D)
        BM = A(22528, 2, D)
        LNG, LNB = A(24576, D), A(25600, D)
        bc_full, bc_done = sem("bc_full"), sem("bc_done")

        def spread_gate(l, part, which):
            b = base("bc", 4)

            def act():
                for dst, src in ((LNG, t["ln_g"]), (LNB, t["ln_b"])):
                    nc.scalar.dma_start(dst, src[l, which:which + 1, :].to_broadcast([P, D])).then_inc(loaded, 16)
                for i in range(4):
                    nc.scalar.wait_ge(bc_full, b + i + 1)
                    nc.scalar.activation(BM[:, i // 2, (i % 2) * 512:(i % 2 + 1) * 512], bank[i][:, :], ACT.Copy).then_inc(bc_done, 1)
                nc.scalar.wait_ge(loaded, loads_now())

            def pe():
                for i in range(4):
                    for j in range(4):
                        k = part * KB + 4 * (i % 2) + j
                        mm = nc.tensor.matmul(bank[i][:, j * P:(j + 1) * P],
                                              MC[:, l, k, i // 2:i // 2 + 1].to_broadcast([P, P]), ident, start=True, stop=True)
                    mm.then_inc(bc_full, 1)

            extra_loads[0] += 2
            n = total_loads_at_start + 16 + 16 * extra_loads[0]

            def loads_now():
                return n
            phase(f"spread{l}_{part}", pe=pe, act=act)

        extra_loads = [0]
        op_full, op_done = sem("op_full"), sem("op_done")

        def out_projection(l, mix, tiles):
            src = t["even_w_out"] if l == 0 else t["odd_w_out"]
            idxs = [chunk(src[:, j * CW:(j + 1) * CW], KB, CW) for j in range(D // CW)]
            jobs = [(j, tl) for j in range(len(idxs)) for tl in tiles]
            b = base("op", len(jobs))
            for i, (j, tl) in enumerate(jobs):
                released[idxs[j]] = (op_full, b + i + 1)

            def pe():
                for i, (j, tl) in enumerate(jobs):
                    if tl == tiles[0]:
                        wait_chunk(nc.tensor, idxs[j])
                    if i >= 8:
                        nc.tensor.wait_ge(op_done, b + i - 7)
                    for k in range(KB):
                        mm = nc.tensor.matmul(bank[i % 8][:, 0:CW], mix(k, tl), slot(idxs[j])[:, k, :],
                                              start=k == 0, stop=k == KB - 1)
                    mm.then_inc(op_full, 1)

            def dve():
                for i, (j, tl) in enumerate(jobs):
                    nc.vector.wait_ge(op_full, b + i + 1)
                    cols = slice(j * CW, (j + 1) * CW)
                    nc.vector.tensor_tensor(OSC[:, tl, cols], bank[i % 8][:, 0:CW], BM[:, int(tl < CT), cols],
                                            ALU.mult).then_inc(op_done, 1)
            phase(f"out_projection{l}", pe=pe, dve=dve)

        ln_var, ln_rstd, ln_mid, ln_done = (sem(f"ln_{x}") for x in ("var", "rstd", "mid", "done"))

        def layer_norm(name, SRC, tiles, scale_by_gate, mod=None):
            b = base("ln", len(tiles))
            V = A(27000, NT, 20)

            def dve():
                for i, tl in enumerate(tiles):
                    s, x, v = SRC[:, tl, :], X[:, tl, :], V[:, tl, :]
                    if scale_by_gate:
                        dv.then(nc.vector.tensor_tensor(s, s, BM[:, int(tl < CT), :], ALU.mult))
                    dv.then(nc.vector.scalar_tensor_tensor(x, x, ALPHA, s, ALU.mult, ALU.add))
                    for j in range(2):
                        dv(nc.vector.bn_stats(v[:, 6 * j:6 * j + 6], x[:, 512 * j:512 * j + 512]))
                    dv.settle()
                    nc.vector.bn_aggr(v[:, 12:14], v[:, 0:12]).then_inc(ln_var, 1)
                    nc.vector.wait_ge(ln_rstd, b + i + 1)
                    dv.then(nc.vector.reciprocal(v[:, 15:16], v[:, 14:15]))
                    nc.vector.tensor_scalar(x, x, v[:, 12:13], v[:, 15:16], ALU.subtract, ALU.mult).then_inc(ln_mid, 1)
                if mod:
                    mod_dve()

            if mod:
                mod_pe, mod_act, mod_dve, _ = modulation(*mod)

            def act():
                for i, tl in enumerate(tiles):
                    nc.scalar.wait_ge(ln_var, b + i + 1)
                    nc.scalar.activation(V[:, tl, 14:15], V[:, tl, 13:14], ACT.Sqrt, bias=C("eps")).then_inc(ln_rstd, 1)
                    if mod:
                        mod_act(i, len(tiles))

            def pool():
                for i, tl in enumerate(tiles):
                    x = X[:, tl, :]
                    nc.gpsimd.wait_ge(ln_mid, b + i + 1)
                    po.then(nc.gpsimd.tensor_tensor(x, x, LNG, ALU.mult))
                    nc.gpsimd.tensor_tensor(x, x, LNB, ALU.add).then_inc(ln_done, 1)

            phase(name, pe=mod_pe if mod else None, act=act, dve=dve, pool=pool)

        AFF = STAT
        SLT = SM(NT, NE)
        RT = SM(3, 8)
        PL, PC = A(6144, LT, NE * CAP_L), A(10240, CT, NE * CAP_C)
        PTL, PTC = A(11264, NE // 2, S_LAT), A(15360, NE // 2, S_CTX)
        YACC = A(0, NT, D)
        rt = {x: sem(f"rt_{x}") for x in ("log", "max", "exp", "aff", "afft", "afftc", "slot", "slt", "sltc", "pt", "ptd")}

        def routing(l, with_ctx, mod=None):
            tiles = list(range(NT)) if with_ctx else list(range(CT, NT))
            nt = len(tiles)
            UT = A(0, KB, TOK)
            o = l
            aff = AFF[:, 0:nt, :]
            lo = 0 if with_ctx else S_CTX
            spans = ([(0, S_CTX, CAP_C)] if with_ctx else []) + [(S_CTX, TOK, CAP_L)]
            AFT, WORK, GT, EQ, CUM = (A(23776 + TOK * i, TOK)[0:NE, :] for i in range(5))
            pairs = [(kind, p) for kind in (["ctx"] if with_ctx else []) + ["lat"] for p in range(NE // 2)]
            bpt = base("pt", len(pairs))
            if mod:
                mod_pe, mod_act, mod_dve, mod_done = modulation(*mod)

            def pe():
                for n, tl in enumerate(tiles):
                    for k in range(KB):
                        mm = nc.tensor.matmul(bank[0][:, n * NE:(n + 1) * NE], UT[:, k, tl * P:(tl + 1) * P],
                                              ROUT[:, l, k * NE:(k + 1) * NE], start=k == 0, stop=k == KB - 1)
                mm.then_inc(rt["log"], 1)
                nc.tensor.wait_ge(rt["aff"], o + 1)
                for n, tl in enumerate(tiles):
                    c = tl * P - (S_CTX if tl >= CT else 0)
                    mm = nc.tensor.transpose(bank[1 + (tl >= CT)][0:NE, c:c + P], aff[:, n, :], ident)
                mm.then_inc(rt["afft"], 1)
                if mod:
                    mod_pe()
                nc.tensor.wait_ge(rt["slot"], o + 1)
                for n, tl in enumerate(tiles):
                    mm = nc.tensor.transpose(bank[3][:, n * NE:(n + 1) * NE], GT[:, tl * P:(tl + 1) * P], ident[0:NE, 0:NE])
                mm.then_inc(rt["slt"], 1)
                if mod:
                    nc.tensor.wait_ge(mod_added, mod_done)
                for i, (kind, p) in enumerate(pairs):
                    pick = C(f"pick_{kind}").rearrange("p (a c) -> p a c", a=NE // 2)[0:NE, p, :]
                    m = pick.shape[1]
                    cols = slice(0, S_CTX) if kind == "ctx" else slice(S_CTX, TOK)
                    n = cols.stop - cols.start
                    if i >= 2:
                        nc.tensor.wait_ge(rt["ptd"], bpt + i - 1)
                    nc.tensor.matmul(bank[4 + 2 * (i % 2)][0:m, 0:n], pick, GT[:, cols], start=True, stop=True)
                    nc.tensor.matmul(bank[5 + 2 * (i % 2)][0:m, 0:n], pick, AFT[:, cols], start=True, stop=True).then_inc(rt["pt"], 1)

            def act():
                nc.scalar.wait_ge(rt["max"], o + 1)
                nc.scalar.activation(aff, aff, ACT.Exp).then_inc(rt["exp"], 1)
                if mod:
                    mod_act()
                for i, (kind, p) in enumerate(pairs):
                    m, n = (2 * CAP_C, S_CTX) if kind == "ctx" else (P, S_LAT)
                    dst = (PTC if kind == "ctx" else PTL)[0:m, p, :]
                    nc.scalar.wait_ge(rt["pt"], bpt + i + 1)
                    nc.scalar.activation(dst, bank[5 + 2 * (i % 2)][0:m, 0:n], ACT.Copy).then_inc(ptc, 1)

            def dve():
                R = RT[:, 0, 0:nt]
                nc.vector.wait_ge(rt["log"], o + 1)
                lg = bank[0][:, 0:nt * NE].rearrange("p (t e) -> p t e", t=nt)
                dv.then(nc.vector.tensor_reduce(R, lg, AX.X, ALU.max))
                nc.vector.tensor_tensor(aff, lg, over_cols(R, NE), ALU.subtract).then_inc(rt["max"], 1)
                nc.vector.wait_ge(rt["exp"], o + 1)
                dv.then(nc.vector.tensor_reduce(R, aff, AX.X, ALU.add))
                dv.then(nc.vector.reciprocal(R, R))
                nc.vector.tensor_tensor(aff, aff, over_cols(R, NE), ALU.mult).then_inc(rt["aff"], 1)
                nc.vector.wait_ge(rt["afft"], o + 1)
                for a, b_, cap in spans:
                    src = bank[1 if a == 0 else 2][0:NE, 0:b_ - a]
                    dv(nc.vector.tensor_copy(AFT[:, a:b_], src))
                    dv.then(nc.vector.tensor_copy(WORK[:, a:b_], src))
                for j, (a, b_, cap) in enumerate(spans):
                    top, T1 = RT[0:NE, 1, :], RT[0:NE, 2, :]
                    for r in range(cap // 8):
                        dv.then(nc.vector.max(top, WORK[:, a:b_]))
                        if r < cap // 8 - 1:
                            dv.then(nc.vector.match_replace(WORK[:, a:b_], top, WORK[:, a:b_], -1.0))
                    thr = top[:, 7:8]
                    dv(nc.vector.tensor_scalar(GT[:, a:b_], AFT[:, a:b_], thr, None, ALU.is_gt))
                    dv.then(nc.vector.tensor_scalar(EQ[:, a:b_], AFT[:, a:b_], thr, None, ALU.is_equal))
                    dv.then(nc.vector.tensor_reduce(T1[:, 0:1], GT[:, a:b_], AX.X, ALU.add))
                    dv.then(nc.vector.tensor_scalar(T1[:, 1:2], T1[:, 0:1], -1.0, float(cap), ALU.mult, ALU.add))
                    dv.then(nc.vector.tensor_tensor_scan(CUM[:, a:b_], one(b_ - a), EQ[:, a:b_], 0.0, ALU.mult, ALU.add))
                    dv.then(nc.vector.scalar_tensor_tensor(EQ[:, a:b_], CUM[:, a:b_], T1[:, 1:2], EQ[:, a:b_], ALU.is_le, ALU.mult))
                    dv.then(nc.vector.tensor_tensor(GT[:, a:b_], GT[:, a:b_], EQ[:, a:b_], ALU.add))
                    dv.then(nc.vector.tensor_tensor_scan(CUM[:, a:b_], one(b_ - a), GT[:, a:b_], 0.0, ALU.mult, ALU.add))
                    dv.then(nc.vector.tensor_tensor(GT[:, a:b_], GT[:, a:b_], CUM[:, a:b_], ALU.mult))
                nc.vector.drain().then_inc(rt["slot"], 1)
                if mod:
                    mod_dve()
                nc.vector.wait_ge(rt["slt"], o + 1)
                slt = bank[3][:, 0:nt * NE].rearrange("p (t e) -> p t e", t=nt)
                dv.then(nc.vector.tensor_copy(SLT[:, 0:nt, :], slt))
                for n, tl in enumerate(tiles):
                    dst, cap = (PC[:, tl, :], CAP_C) if tl < CT else (PL[:, tl - CT, :], CAP_L)
                    slots = C("slots")[:, 0:cap].rearrange("p (a c) -> p a c", a=1).to_broadcast([P, NE, cap])
                    nc.vector.tensor_tensor(dst.rearrange("p (e c) -> p e c", e=NE), slots, over_cols(SLT[:, n, :], cap), ALU.is_equal)
                for i, (kind, p) in enumerate(pairs):
                    m, n = (2 * CAP_C, S_CTX) if kind == "ctx" else (P, S_LAT)
                    dst = (PTC if kind == "ctx" else PTL)[0:m, p, :]
                    nc.vector.wait_ge(ptc, bpt + i + 1)
                    nc.vector.scalar_tensor_tensor(dst, bank[4 + 2 * (i % 2)][0:m, 0:n], C(f"slot_{kind}")[0:m, :], dst,
                                                   ALU.is_equal, ALU.mult).then_inc(rt["ptd"], 1)

            phase(f"routing{l}", pe=pe, act=act, dve=dve)

        ptc = sem("ptc")

        def one(n):
            return C("ones")[0:NE, 0:1].to_broadcast([NE, n])

        ex = {x: sem(f"ex_{x}") for x in ("gather", "xe", "gate", "up", "silu", "hid", "down", "dl", "dc",
                                          "scatter", "added", "ptcur")}
        PAIR_CHUNKS = 2 * 3 * D // CW
        ex_base = {x: 0 for x in ex}
        slot_free = sem("slot_free")

        def expert_loop(l, with_ctx):
            M = CAP_L + (CAP_C if with_ctx else 0)
            NP = NE // 2
            first = n_chunks[0]
            assert PAIR_CHUNKS % RING == 0
            n_chunks[0] += NP * PAIR_CHUNKS
            XE = A(17408, KB, 2 * M)
            SIL = [A(18944 + 2 * M * i, 2, M) for i in range(2)]
            HT = [A(19328 + KB * M * i, KB, M) for i in range(2)]
            YEL, YEC, PTCUR = A(20864, D), A(21888, D), A(22912, S_LAT + S_CTX)
            outs = ([(tl, hf) for tl in range(CT) for hf in range(2)] if with_ctx else []) + \
                   [(tl, hf) for tl in range(CT, NT) for hf in range(2)]
            NS = len(outs)
            per = dict(gather=KB, xe=KB, gate=8, up=8, silu=8, hid=8, down=8, dl=8, dc=8 if with_ctx else 0,
                       scatter=NS, added=NS, ptcur=2 if with_ctx else 1)
            credit = dict(xe=2, silu=2, hid=2, dl=2, dc=2 if with_ctx else 0, added=2)
            start = {x: ex_base[x] for x in ex}
            for x in ex:
                ex_base[x] += credit.get(x, 0) + NP * per[x]

            def at(x, i, n):
                return start[x] + n + i * per[x]

            def source(i, j):
                e, r = j // 12, j % 12
                w, c = ((("moe_w_gate", "moe_w_up")[r % 2], r // 2) if r < 8 else ("moe_w_down", r - 8))
                return w, e, c

            def chunk_free(sp, i, j):
                jj, ii = j - RING, i
                if jj < 0:
                    jj, ii = jj + PAIR_CHUNKS, i - 1
                e, r = jj // 12, jj % 12
                if r >= 8:
                    sp.wait_ge(ex["down"], at("down", ii, 4 * e + r - 7))
                else:
                    x = ("gate", "up")[r % 2]
                    sp.wait_ge(ex[x], at(x, ii, 4 * e + r // 2 + 1))

            def load(sp, i, j, free=None):
                w, e, c = source(i, j)
                s = (first + j) % RING
                flat = t[w].rearrange("l e (k p) n -> (l e) p k n", p=P)
                src = flat[bass.ds(l * NE + 2 * i + e, 1), :, :, c * CW:(c + 1) * CW].rearrange("a p k n -> (a p) k n")
                if free:
                    free()
                    sp.sem_inc(slot_free, 1)
                sp.dma_start(slot(s), src).then_inc(w_full[s], 16)

            def stream(sp):
                for j in range(RING):
                    idx = first + j
                    if idx - RING in released:
                        sp.wait_ge(*released[idx - RING])
                    load(sp, 0, j)
                with sp.Fori(0, NP - 1) as i:
                    for j in range(PAIR_CHUNKS):
                        jj, ii = (j + RING, i) if j + RING < PAIR_CHUNKS else (j + RING - PAIR_CHUNKS, i + 1)
                        load(sp, ii, jj, lambda: chunk_free(sp, ii, jj))
                for j in range(RING, PAIR_CHUNKS):
                    chunk_free(sp, NP - 1, j)
                    load(sp, NP - 1, j)

            chunks.append((first, stream, None, None))
            for j in range(PAIR_CHUNKS - RING, PAIR_CHUNKS):
                e, r = j // 12, j % 12
                x = "down" if r >= 8 else ("gate", "up")[r % 2]
                n = 4 * e + (r - 7 if r >= 8 else r // 2 + 1)
                released[first + (NP - 1) * PAIR_CHUNKS + j] = (ex[x], at(x, NP - 1, n))

            def wait_w(i, j):
                s = (first + j) % RING
                nc.tensor.wait_ge(w_full[s], 16 * ((first + j) // RING + 1) + i * (16 * PAIR_CHUNKS // RING))

            def wslot(j):
                return slot(first + j)

            def scatter_steps(q):
                return range(q * NS // 8, (q + 1) * NS // 8)

            def pe():
                def gather(i, k):
                    nc.tensor.wait_ge(ex["xe"], at("xe", i, k + 1))
                    bk = bank[k % 2]
                    for n in range(LT):
                        mm = nc.tensor.matmul(bk[:, 0:2 * CAP_L], X[:, CT + n, k * P:(k + 1) * P],
                                              PL[:, n, bass.ds(i * (2 * CAP_L), 2 * CAP_L)], start=n == 0, stop=n == LT - 1)
                    if with_ctx:
                        for n in range(CT):
                            mm = nc.tensor.matmul(bk[:, 2 * CAP_L:2 * M], X[:, n, k * P:(k + 1) * P],
                                                  PC[:, n, bass.ds(i * (2 * CAP_C), 2 * CAP_C)], start=n == 0, stop=n == CT - 1)
                    mm.then_inc(ex["gather"], 1)

                def scatter(i, n):
                    tl, hf = outs[n]
                    if n == 0:
                        nc.tensor.wait_ge(ex["dl"], at("dl", i, 8 + 2))
                        if with_ctx:
                            nc.tensor.wait_ge(ex["dc"], at("dc", i, 8 + 2))
                        nc.tensor.wait_ge(ex["ptcur"], at("ptcur", i, per["ptcur"]))
                    nc.tensor.wait_ge(ex["added"], at("added", i, n + 1))
                    if tl < CT:
                        w, y = PTCUR[0:2 * CAP_C, S_LAT + tl * P:S_LAT + (tl + 1) * P], YEC[0:2 * CAP_C, :]
                    else:
                        w, y = PTCUR[:, (tl - CT) * P:(tl - CT + 1) * P], YEL
                    nc.tensor.matmul(bank[6 + n % 2][:, :], w, y[:, hf * 512:(hf + 1) * 512], start=True,
                                     stop=True).then_inc(ex["scatter"], 1)

                def pair(i, first_pair, last_pair):
                    nc.tensor.wait_ge(ex["xe"], at("xe", i, KB + 2))
                    for e in range(2):
                        xe = XE[:, :, e * M:(e + 1) * M]
                        for c in range(4):
                            n = 4 * e + c
                            for w, x, free in (("gate", 2, "silu"), ("up", 4, "hid")):
                                j = 12 * e + 2 * c + (w == "up")
                                wait_w(i, j)
                                nc.tensor.wait_ge(ex[free], at(free, i, n + 1))
                                bk = bank[x + n % 2]
                                for f in range(2):
                                    for k in range(KB):
                                        mm = nc.tensor.matmul(bk[:, f * M:(f + 1) * M], wslot(j)[:, k, f * P:(f + 1) * P],
                                                              xe[:, k, :], start=k == 0, stop=k == KB - 1)
                                mm.then_inc(ex[w], 1)
                                if e == 0 and not first_pair:
                                    for m in scatter_steps(2 * c + (w == "up")):
                                        scatter(i - 1, m)
                        nc.tensor.wait_ge(ex["hid"], at("hid", i, 4 * e + 4 + 2))
                        for c in range(4):
                            n, j = 4 * e + c, 12 * e + 8 + c
                            wait_w(i, j)
                            nc.tensor.wait_ge(ex["dl"], at("dl", i, n + 1))
                            if with_ctx:
                                nc.tensor.wait_ge(ex["dc"], at("dc", i, n + 1))
                            if n < 2:
                                nc.tensor.wait_ge(ex["added"], at("added", i, 1 + n))
                            for f in range(KB):
                                mm = nc.tensor.matmul(bank[6 + n % 2][0:M, 0:CW], HT[e][:, f, :], wslot(j)[:, f, :],
                                                      start=f == 0, stop=f == KB - 1)
                            mm.then_inc(ex["down"], 1)
                            if e == 1 and not last_pair:
                                gather(i + 1, 2 * c)
                                gather(i + 1, 2 * c + 1)

                for k in range(KB):
                    gather(0, k)
                pair(0, True, False)
                with nc.tensor.Fori(1, NP - 1) as i:
                    pair(i, False, False)
                pair(NP - 1, False, True)
                for n in range(NS):
                    scatter(NP - 1, n)

            def act():
                for x in ("silu", "dl"):
                    nc.scalar.sem_inc(ex[x], credit[x])
                with nc.scalar.Fori(0, NP) as i:
                    for e in range(2):
                        for c in range(4):
                            n = 4 * e + c
                            nc.scalar.wait_ge(ex["gate"], at("gate", i, n + 1))
                            nc.scalar.wait_ge(ex["hid"], at("hid", i, n + 1))
                            nc.scalar.activation(SIL[n % 2], bank[2 + n % 2][:, 0:2 * M], ACT.Silu).then_inc(ex["silu"], 1)
                        for c in range(4):
                            n = 4 * e + c
                            nc.scalar.wait_ge(ex["down"], at("down", i, n + 1))
                            if n == 0:
                                nc.scalar.wait_ge(ex["added"], at("added", i, 2))
                            nc.scalar.activation(YEL[e * CAP_L:(e + 1) * CAP_L, c * CW:(c + 1) * CW],
                                                 bank[6 + n % 2][0:CAP_L, 0:CW], ACT.Copy).then_inc(ex["dl"], 1)

            def dve():
                for x in ("xe", "hid", "dc", "added"):
                    if credit[x]:
                        nc.vector.sem_inc(ex[x], credit[x])
                def gathered(i, k):
                    nc.vector.wait_ge(ex["gather"], at("gather", i, k + 1))
                    xe = XE[:, k, :].rearrange("p (e m) -> p e m", e=2)
                    bk = bank[k % 2]
                    s, o = 4 * KB + k, 3 * KB + k
                    ins = nc.vector.tensor_scalar(xe[:, :, 0:CAP_L], bk[:, 0:2 * CAP_L].rearrange("p (e m) -> p e m", e=2),
                                                  MC[:, l, s, 0:1], MC[:, l, o, 0:1], ALU.mult, ALU.add)
                    if with_ctx:
                        ins = nc.vector.tensor_scalar(xe[:, :, CAP_L:M], bk[:, 2 * CAP_L:2 * M].rearrange("p (e m) -> p e m", e=2),
                                                      MC[:, l, s, 1:2], MC[:, l, o, 1:2], ALU.mult, ALU.add)
                    ins.then_inc(ex["xe"], 1)

                def add(i, n):
                    tl, hf = outs[n]
                    nc.vector.wait_ge(ex["scatter"], at("scatter", i, n + 1))
                    y = YACC[:, tl, hf * 512:(hf + 1) * 512]
                    nc.vector.tensor_tensor(y, y, bank[6 + n % 2][:, :], ALU.add).then_inc(ex["added"], 1)

                def pair(i, first_pair, last_pair):
                    for e in range(2):
                        for c in range(4):
                            n = 4 * e + c
                            nc.vector.wait_ge(ex["up"], at("up", i, n + 1))
                            nc.vector.wait_ge(ex["silu"], at("silu", i, n + 1 + 2))
                            nc.vector.tensor_tensor(HT[e][:, 2 * c:2 * c + 2, :], SIL[n % 2],
                                                    bank[4 + n % 2][:, 0:2 * M].rearrange("p (f m) -> p f m", f=2),
                                                    ALU.mult).then_inc(ex["hid"], 1)
                            if e == 0 and not first_pair:
                                for m in (*scatter_steps(2 * c), *scatter_steps(2 * c + 1)):
                                    add(i - 1, m)
                        for c in range(4):
                            n = 4 * e + c
                            if with_ctx:
                                nc.vector.wait_ge(ex["down"], at("down", i, n + 1))
                                nc.vector.tensor_copy(YEC[e * CAP_C:(e + 1) * CAP_C, c * CW:(c + 1) * CW],
                                                      bank[6 + n % 2][CAP_L:M, 0:CW]).then_inc(ex["dc"], 1)
                            if e == 1 and not last_pair:
                                gathered(i + 1, 2 * c)
                                gathered(i + 1, 2 * c + 1)

                for k in range(KB):
                    gathered(0, k)
                pair(0, True, False)
                with nc.vector.Fori(1, NP - 1) as i:
                    pair(i, False, False)
                pair(NP - 1, False, True)
                for n in range(NS):
                    add(NP - 1, n)

            def pool():
                with nc.gpsimd.Fori(0, NP) as i:
                    nc.gpsimd.wait_ge(ex["added"], at("added", i, 2))
                    if with_ctx:
                        nc.gpsimd.tensor_copy(PTCUR[0:2 * CAP_C, S_LAT:S_LAT + S_CTX],
                                              PTC[0:2 * CAP_C, bass.ds(i, 1), :].rearrange("p a n -> p (a n)")).then_inc(ex["ptcur"], 1)
                    nc.gpsimd.tensor_copy(PTCUR[:, 0:S_LAT], PTL[:, bass.ds(i, 1), :].rearrange("p a n -> p (a n)")).then_inc(ex["ptcur"], 1)

            phase(f"experts{l}", pe=pe, act=act, dve=dve, pool=pool)

        def clear_y(with_ctx):
            def pool():
                nc.gpsimd.memset(YACC, 0.0)
            phase("clear", pool=pool)

        start(*modulation(0, 0, NMOD * D // CW, (0, 1, 2), 0)[:3])
        modulated_transpose(0, 1, 0)
        mla_latents()
        mla_norm()
        mla_up()
        mla_rope()
        mla_attention()
        keep_mla()
        gdn_qkv()
        gdn_gate_inputs()
        gdn_norm()
        gdn_cumsum()
        gdn_tokens()
        gdn_scan()
        MIX0 = A(0, H, TOK)
        gated_norm(0, OG, SZ, A(21900, NT, HW), MIX0, list(range(NT)))
        MIX1 = A(3072, H, TOK)

        def fetch_mla():
            def act():
                nc.scalar.dma_start(MIX1, t["mla_mix"].rearrange("p (h n) -> p h n", h=H)).then_inc(stored, 16)
                nc.scalar.wait_ge(stored, 32)
            phase("fetch_mla", act=act)
        fetch_mla()
        spread_gate(0, 2, 0)
        out_projection(0, lambda k, tl: (MIX0, MIX1)[k // H][:, k % H, tl * P:(tl + 1) * P], list(range(NT)))
        layer_norm("norm0", OSC, list(range(NT)), False, mod=(1, MOD1_CUTS[0], MOD1_CUTS[1], (0, 1, 2), 27200))
        modulated_transpose(0, 4, 3)
        routing(0, True, mod=(1, MOD1_CUTS[1], NMOD * D // CW, (5, 6, 7), 17408))
        clear_y(True)
        expert_loop(0, True)
        spread_gate(0, 5, 1)
        layer_norm("norm1", YACC, list(range(NT)), True)
        modulated_transpose(1, 1, 0)
        na_projections()
        na_attention()
        hgrn_projections()
        hgrn_scan()
        MIXH = A(0, H, S_LAT)
        gated_norm(1, OH, SG, A(2048, LT, HW), MIXH, list(range(LT)))
        spread_gate(1, 2, 0)
        out_projection(1, lambda k, tl: (MIXN, MIXH)[k // H][:, k % H, (tl - CT) * P:(tl - CT + 1) * P], list(range(CT, NT)))
        layer_norm("norm2", OSC, list(range(CT, NT)), False)
        modulated_transpose(1, 4, 3, with_ctx=False)
        routing(1, False)
        clear_y(False)
        expert_loop(1, False)
        spread_gate(1, 5, 1)
        layer_norm("norm3", YACC, list(range(CT, NT)), True)

        if upto is not None:
            names = [p[0] for p in phases]
            del phases[names.index(upto) + 1:]

        dump_aps = {"X": X, "UT": A(0, KB, TOK), "MC": MC, "P34": P34, "KR": KR, "QN": QN, "QR": QR, "KN": KN, "VM": VM,
                    "MIXM": MIXM, "QT": QT, "KT": KT, "VT": VT, "SZ": SZ, "G": G, "BETA": BETA, "OG": OG, "MIX0": MIX0,
                    "MIX1": MIX1, "OSC": OSC, "YACC": YACC, "AFF": AFF, "SLT": SLT, "MIXN": MIXN, "OH": OH, "MIXH": MIXH,
                    "PL": PL, "PC": PC, "PTL": PTL, "PTC": PTC, "BM": BM, "AB": AB, "EG": EG, "EL": EL, "ET": ET,
                    "NQ": NQ, "NK": NK, "NV": NV, "CC": CC, "KTOK": KTOK, "VTOK": VTOK, "GS": GS, "TOT1": TOT1, "TOT2": TOT2, "XE": A(17408, KB, 192), "HT": A(19328, 2, KB, 96), "YEL": A(20864, D),
                    "YEC": A(21888, D), "PTCUR": A(22912, 768)}

        if upto is not None:
            dumped = sem("dumped")
        block = es.enter_context(nc.Block())
        ends = len(phases)

        def run(eng, which):
            for n, (name, *parts) in enumerate(phases):
                if parts[which] is not None:
                    parts[which]()
                eng.drain().then_inc(phase_done, 1)
                eng.wait_ge(phase_done, 4 * (n + 1))

        @block.tensor
        def _(pe):
            run(nc.tensor, 0)

        @block.scalar
        def _(act):
            run(nc.scalar, 1)

        @block.vector
        def _(dve):
            run(nc.vector, 2)

        @block.gpsimd
        def _(pool):
            run(nc.gpsimd, 3)

        @block.sync
        def _(sp):
            for idx, src, k, n in chunks:
                if idx >= chunks_until[ends - 1]:
                    break
                if callable(src):
                    src(nc.sync)
                    continue
                if idx >= RING:
                    nc.sync.wait_ge(*released[idx - RING])
                nc.sync.dma_start(slot(idx, k, n), src.rearrange("(k p) n -> p k n", p=P)).then_inc(w_full[idx % RING], 16)
            nc.sync.wait_ge(phase_done, 4 * ends)
            n = 0
            if upto is None:
                nc.sync.dma_start(t["out"].rearrange("o (t p) d -> p (o t) d", p=P), X[:, CT:NT, :]).then_inc(stored, 16)
                nc.sync.wait_ge(stored, 16 * 3)
            else:
                for name in dumps:
                    ap = dump_aps[name]
                    nc.sync.dma_start(t["dump_" + name], ap).then_inc(dumped, 16)
                nc.sync.wait_ge(dumped, 16 * len(dumps))


_WHOLE = ["x", "ctx", "w_mod", "ln_g", "ln_b", "even_w_in", "gdn_a_log", "gdn_dt_bias", "gdn_norm", "mla_w_uq", "mla_w_ukv",
          "even_w_out", "odd_w_in", "hg_norm", "odd_w_out", "moe_router", "moe_w_gate", "moe_w_up", "moe_w_down"]


def lay_out(inp):
    a = {n: np.ascontiguousarray(inp[n]) for n in _WHOLE}

    def columns(v, n):
        return np.ascontiguousarray(np.asarray(v).reshape(n, P).T)

    a["cc"] = np.ascontiguousarray(np.stack([columns(inp["c"], KB), columns(inp["c_ctx"], KB)], -1).reshape(P, -1))
    a["b_mod_cols"] = columns(inp["b_mod"], DEPTH * NMOD * KB)
    a["q_gain_cols"] = columns(inp["mla_q_norm"], 2)
    a["kv_gain_cols"] = columns(inp["mla_kv_norm"], 2)
    a["hg_lb_cols"] = columns(inp["hg_lb"], 2 * H)
    conv = np.asarray(inp["gdn_conv"])[0]
    a["conv_cols"] = np.ascontiguousarray(conv.reshape(TAPS, 12, P).transpose(2, 1, 0).reshape(P, -1))
    a["consts"] = CONST
    rpb = np.asarray(inp["na_rpb"])[0]
    w = np.arange(GRID)
    c0 = np.clip(w - NA_KW // 2, 0, GRID - NA_KW)
    ok = (w[None] >= c0[:, None]) & (w[None] < c0[:, None] + NA_KW)
    off = np.clip(w[None] - w[:, None] + NA_KW - 1, 0, 2 * NA_KW - 2)
    tables = np.full((P, NA_H, 16, GRID), NEG, rpb.dtype)
    spread = np.where(ok[:, None, None], rpb[:, :, off].transpose(2, 0, 1, 3), rpb.dtype.type(NEG))
    tables[0:GRID, :, 0:15] = spread
    tables[GRID:, :, 1:16] = spread
    a["rpb_tables"] = np.ascontiguousarray(tables.reshape(P, NA_H, -1))
    return a


def declare(nc, arrays):
    t = {n: nc.dram_tensor(f"in_{n}_dram", a.shape, mybir.dt.from_np(a.dtype), kind="ExternalInput").ap()
         for n, a in arrays.items()}
    for n in ("even_w_in", "mla_w_uq", "mla_w_ukv", "even_w_out", "odd_w_in", "odd_w_out"):
        t[n] = t[n][0]
    t["mla_mix"] = nc.dram_tensor("mla_mix_dram", (P, H * TOK), F32, kind="Internal").ap()
    return t


def kernel(**inputs):
    import concourse.bacc as _bacc
    from concourse.bass_utils import run_bass_kernel_spmd as _run

    arrays = lay_out(inputs)
    nc = _bacc.Bacc("TRN2", target_bir_lowering=False, num_devices=1)
    t = declare(nc, arrays)
    t["out"] = nc.dram_tensor("out_0_dram", (1, S_LAT, D), F32, kind="ExternalOutput").ap()
    program(nc, t)
    r = _run(nc, [{f"in_{n}_dram": a for n, a in arrays.items()}], core_ids=[0])
    return r.results[0]["out_0_dram"]
```
